# Optimizing a Trainium2 kernel written in Bass

```python
import math
import jax, jax.numpy as jnp
from jax import lax
import numpy as np

D_MODEL = 1024
BATCH = 1
SEQ = 1024
DEPTH = 1

CHUNK = 64
Q_BLOCK = 128
EPS = 1e-6

GDN_HEADS = 4
GDN_HEAD_DIM = 128
GDN_WIDTH = GDN_HEADS * GDN_HEAD_DIM
CONV_WIDTH = 4

POOL_GROUPS = 4
POOL_GROUP_DIM = 64
POOL_WIDTH = POOL_GROUPS * POOL_GROUP_DIM
POOL_WINDOWS = (2, 4, 8, 16)

MLA_HEADS = 4
MLA_NOPE = 64
MLA_ROPE = 32
MLA_QK_DIM = MLA_NOPE + MLA_ROPE
MLA_V = 64
MLA_Q_RANK = 256
MLA_KV_RANK = 128
MLA_WIDTH = MLA_HEADS * MLA_V
ROPE_THETA = 10000.0

D_MIX = GDN_WIDTH + POOL_WIDTH + MLA_WIDTH

OFF_QKV = 0
OFF_GATE = OFF_QKV + 3 * GDN_WIDTH
OFF_A = OFF_GATE + GDN_WIDTH
OFF_B = OFF_A + GDN_HEADS
OFF_POOL = OFF_B + GDN_HEADS
OFF_CQ = OFF_POOL + POOL_WIDTH
OFF_CKV = OFF_CQ + MLA_Q_RANK
OFF_KR = OFF_CKV + MLA_KV_RANK
D_IN = OFF_KR + MLA_ROPE

FFN_HIDDEN = ((8 * D_MODEL // 3 + 255) // 256) * 256

kernel_name = "hybrid_gdn_pool_mla_block"

def rms_norm(x, g):
    xf = x.astype(jnp.float32)
    y = xf * lax.rsqrt(jnp.mean(xf * xf, axis=-1, keepdims=True) + EPS)
    return (y * g.astype(jnp.float32)).astype(x.dtype)

def l2_normalize(x):
    xf = x.astype(jnp.float32)
    return xf * lax.rsqrt(jnp.sum(xf * xf, axis=-1, keepdims=True) + EPS)

def causal_depthwise_conv(x, w):
    c = x.shape[-1]
    return lax.conv_general_dilated(
        x, w[:, None, :].astype(x.dtype), window_strides=(1,),
        padding=[(CONV_WIDTH - 1, 0)], dimension_numbers=("NWC", "WIO", "NWC"),
        feature_group_count=c)

def rotary(x, cos, sin):
    x1, x2 = jnp.split(x.astype(jnp.float32), 2, axis=-1)
    return jnp.concatenate([x1 * cos - x2 * sin, x2 * cos + x1 * sin], axis=-1).astype(x.dtype)

def gated_delta_rule(q, k, v, g, beta):
    b, s, h, dk = q.shape
    dv = v.shape[-1]
    n = s // CHUNK

    def blocks(t):
        return t.reshape(b, n, CHUNK, h, t.shape[-1]).transpose(0, 1, 3, 2, 4)

    q, k, v = blocks(q), blocks(k), blocks(v)
    g = jnp.cumsum(g.reshape(b, n, CHUNK, h).transpose(0, 1, 3, 2), axis=-1)
    beta = beta.reshape(b, n, CHUNK, h).transpose(0, 1, 3, 2)

    idx = jnp.arange(CHUNK)
    causal = idx[:, None] >= idx[None, :]
    strict = idx[:, None] > idx[None, :]
    diff = g[..., :, None] - g[..., None, :]
    decay = jnp.where(causal, jnp.exp(jnp.where(causal, diff, 0.0)), 0.0)

    k_beta = k * beta[..., None]
    v_beta = v * beta[..., None]
    a_low = jnp.where(strict, jnp.einsum('bnhcd,bnhed->bnhce', k_beta, k) * decay, 0.0)
    ia = a_low + jnp.eye(CHUNK, dtype=jnp.float32)
    w = lax.linalg.triangular_solve(ia, k_beta * jnp.exp(g)[..., None], left_side=True,
                                    lower=True, unit_diagonal=True)
    u = lax.linalg.triangular_solve(ia, v_beta, left_side=True, lower=True, unit_diagonal=True)
    attn_intra = jnp.einsum('bnhcd,bnhed->bnhce', q, k) * decay
    q_dec = q * jnp.exp(g)[..., None]
    g_last = g[..., -1]
    k_dec = k * jnp.exp(g_last[..., None] - g)[..., None]

    xs = tuple(jnp.swapaxes(t, 0, 1) for t in (q_dec, w, u, attn_intra, k_dec, g_last))

    def step(state, inp):
        q_i, w_i, u_i, attn_i, kd_i, gl_i = inp
        v_new = u_i - jnp.einsum('bhcd,bhde->bhce', w_i, state)
        o_i = jnp.einsum('bhcd,bhde->bhce', q_i, state) + jnp.einsum('bhce,bhef->bhcf', attn_i, v_new)
        state = state * jnp.exp(gl_i)[..., None, None] + jnp.einsum('bhcd,bhce->bhde', kd_i, v_new)
        return state, o_i

    s0 = jnp.zeros((b, h, dk, dv), jnp.float32)
    _, o = lax.scan(step, s0, xs)
    return o.transpose(1, 0, 3, 2, 4).reshape(b, s, h, dv)

def multiscale_pool(xb, pool_w, pool_scale):
    b, s, _ = xb.shape
    xg = xb.astype(jnp.float32).reshape(b, s, POOL_GROUPS, POOL_GROUP_DIM)
    cs0 = jnp.concatenate([jnp.zeros((b, 1, POOL_GROUPS, POOL_GROUP_DIM), jnp.float32),
                           jnp.cumsum(xg, axis=1)], axis=1)
    t = jnp.arange(s)
    pooled = []
    for gi, win in enumerate(POOL_WINDOWS):
        start = jnp.maximum(t + 1 - win, 0)
        total = cs0[:, 1:, gi] - jnp.take(cs0[:, :, gi], start, axis=1)
        count = jnp.minimum(t + 1, win).astype(jnp.float32)
        pooled.append(total / count[None, :, None])
    pooled = jnp.stack(pooled, axis=2)
    mixed = jnp.einsum('bsgc,gcd->bsgd', pooled - xg, pool_w.astype(jnp.float32))
    return (mixed.reshape(b, s, POOL_WIDTH) * pool_scale.astype(jnp.float32)).astype(xb.dtype)

def chunk_causal_attention(q, k, v):
    b, s, h, dqk = q.shape
    qf = q.astype(jnp.float32) * (dqk ** -0.5)
    kf = k.astype(jnp.float32)
    vf = v.astype(jnp.float32)
    outs = []
    for qs in range(0, s, Q_BLOCK):
        end = qs + Q_BLOCK
        scores = jnp.einsum('bqhd,bkhd->bhqk', qf[:, qs:end], kf[:, :end])
        q_chunk = (qs + jnp.arange(Q_BLOCK)) // CHUNK
        k_chunk = jnp.arange(end) // CHUNK
        mask = k_chunk[None, :] <= q_chunk[:, None]
        p = jax.nn.softmax(jnp.where(mask, scores, -jnp.inf), axis=-1)
        outs.append(jnp.einsum('bhqk,bkhd->bqhd', p, vf[:, :end]))
    return jnp.concatenate(outs, axis=1).astype(q.dtype)

def hybrid_mixer(hn, cos, sin, w_in, conv_w, a_log, dt_bias, gdn_out_norm, pool_w, pool_scale,
                 q_a_norm, w_uq, kv_a_norm, w_ukv, q_norm, k_norm, w_out):
    b, s, _ = hn.shape
    proj = hn @ w_in

    qkv = jax.nn.silu(causal_depthwise_conv(proj[..., OFF_QKV:OFF_GATE], conv_w))
    q_a, k_a, v_a = jnp.split(qkv, 3, axis=-1)
    q_a = l2_normalize(q_a.reshape(b, s, GDN_HEADS, GDN_HEAD_DIM)) * (GDN_HEAD_DIM ** -0.5)
    k_a = l2_normalize(k_a.reshape(b, s, GDN_HEADS, GDN_HEAD_DIM))
    v_a = v_a.reshape(b, s, GDN_HEADS, GDN_HEAD_DIM).astype(jnp.float32)
    gate = proj[..., OFF_GATE:OFF_A].astype(jnp.float32).reshape(b, s, GDN_HEADS, GDN_HEAD_DIM)
    a_in = proj[..., OFF_A:OFF_B].astype(jnp.float32)
    b_in = proj[..., OFF_B:OFF_POOL].astype(jnp.float32)
    beta = jax.nn.sigmoid(b_in)
    g = -jnp.exp(a_log.astype(jnp.float32)) * jax.nn.softplus(a_in + dt_bias.astype(jnp.float32))
    o_a = gated_delta_rule(q_a, k_a, v_a, g, beta)
    o_a = (rms_norm(o_a, gdn_out_norm) * jax.nn.silu(gate)).reshape(b, s, GDN_WIDTH).astype(hn.dtype)

    o_b = multiscale_pool(proj[..., OFF_POOL:OFF_CQ], pool_w, pool_scale)

    c_q = rms_norm(proj[..., OFF_CQ:OFF_CKV], q_a_norm)
    q_c = (c_q @ w_uq).reshape(b, s, MLA_HEADS, MLA_QK_DIM)
    c_kv = rms_norm(proj[..., OFF_CKV:OFF_KR], kv_a_norm)
    kv = (c_kv @ w_ukv).reshape(b, s, MLA_HEADS, MLA_NOPE + MLA_V)
    k_nope, v_c = kv[..., :MLA_NOPE], kv[..., MLA_NOPE:]
    k_rope = jnp.broadcast_to(proj[..., OFF_KR:D_IN][:, :, None, :], (b, s, MLA_HEADS, MLA_ROPE))
    k_c = jnp.concatenate([k_nope, k_rope], axis=-1)
    q_c = rms_norm(q_c, q_norm)
    k_c = rms_norm(k_c, k_norm)
    q_c = jnp.concatenate([q_c[..., :MLA_NOPE], rotary(q_c[..., MLA_NOPE:], cos, sin)], axis=-1)
    k_c = jnp.concatenate([k_c[..., :MLA_NOPE], rotary(k_c[..., MLA_NOPE:], cos, sin)], axis=-1)
    o_c = chunk_causal_attention(q_c, k_c, v_c).reshape(b, s, MLA_WIDTH)

    return jnp.concatenate([o_a, o_b, o_c], axis=-1) @ w_out

def setup_inputs(seed: int = 0) -> dict:
    key = jax.random.key(seed)
    ks = jax.random.split(key, 24)
    f32 = jnp.float32

    def nrm(k, shape, scale):
        return jax.random.normal(k, shape, f32) * scale

    def gain(k, shape):
        return 1.0 + 0.02 * jax.random.normal(k, shape, f32)

    x = jax.random.normal(ks[0], (BATCH, SEQ, D_MODEL), f32)
    offsets = jax.random.randint(ks[1], (BATCH, 1), 0, 64, dtype=jnp.int32) * CHUNK
    positions = (jnp.arange(SEQ, dtype=jnp.int32)[None, :] + offsets).astype(jnp.int32)
    dt = jnp.exp(jax.random.uniform(ks[6], (DEPTH, GDN_HEADS), f32, math.log(1e-3), math.log(1e-1)))
    return {
        "x": x,
        "positions": positions,
        "attn_norm": gain(ks[2], (DEPTH, D_MODEL)),
        "w_in": nrm(ks[3], (DEPTH, D_MODEL, D_IN), D_MODEL ** -0.5),
        "conv_w": nrm(ks[4], (DEPTH, CONV_WIDTH, 3 * GDN_WIDTH), CONV_WIDTH ** -0.5),
        "a_log": jnp.log(jax.random.uniform(ks[5], (DEPTH, GDN_HEADS), f32, 1.0, 16.0)),
        "dt_bias": dt + jnp.log(-jnp.expm1(-dt)),
        "gdn_out_norm": gain(ks[7], (DEPTH, GDN_HEAD_DIM)),
        "pool_w": nrm(ks[8], (DEPTH, POOL_GROUPS, POOL_GROUP_DIM, POOL_GROUP_DIM), POOL_GROUP_DIM ** -0.5),
        "pool_scale": 1.0 + 0.1 * jax.random.normal(ks[9], (DEPTH, POOL_WIDTH), f32),
        "q_a_norm": gain(ks[10], (DEPTH, MLA_Q_RANK)),
        "w_uq": nrm(ks[11], (DEPTH, MLA_Q_RANK, MLA_HEADS * MLA_QK_DIM), MLA_Q_RANK ** -0.5),
        "kv_a_norm": gain(ks[12], (DEPTH, MLA_KV_RANK)),
        "w_ukv": nrm(ks[13], (DEPTH, MLA_KV_RANK, MLA_HEADS * (MLA_NOPE + MLA_V)), MLA_KV_RANK ** -0.5),
        "q_norm": gain(ks[14], (DEPTH, MLA_QK_DIM)),
        "k_norm": gain(ks[15], (DEPTH, MLA_QK_DIM)),
        "w_out": nrm(ks[16], (DEPTH, D_MIX, D_MODEL), (D_MIX * 2 * DEPTH) ** -0.5),
        "ffn_norm": gain(ks[17], (DEPTH, D_MODEL)),
        "w_gate_up": nrm(ks[18], (DEPTH, D_MODEL, 2 * FFN_HIDDEN), D_MODEL ** -0.5),
        "w_down": nrm(ks[19], (DEPTH, FFN_HIDDEN, D_MODEL), (FFN_HIDDEN * 2 * DEPTH) ** -0.5),
    }

def reference(x, positions, attn_norm, w_in, conv_w, a_log, dt_bias, gdn_out_norm, pool_w, pool_scale,
              q_a_norm, w_uq, kv_a_norm, w_ukv, q_norm, k_norm, w_out, ffn_norm, w_gate_up, w_down):
    inv_freq = ROPE_THETA ** (-jnp.arange(0, MLA_ROPE, 2, dtype=jnp.float32) / MLA_ROPE)
    ang = positions.astype(jnp.float32)[..., None] * inv_freq
    cos = jnp.cos(ang)[:, :, None, :]
    sin = jnp.sin(ang)[:, :, None, :]

    for l in range(DEPTH):
        hn = rms_norm(x, attn_norm[l])
        x = x + hybrid_mixer(hn, cos, sin, w_in[l], conv_w[l], a_log[l], dt_bias[l], gdn_out_norm[l],
                             pool_w[l], pool_scale[l], q_a_norm[l], w_uq[l], kv_a_norm[l], w_ukv[l],
                             q_norm[l], k_norm[l], w_out[l])
        hf = rms_norm(x, ffn_norm[l])
        gate_f, up = jnp.split(hf @ w_gate_up[l], 2, axis=-1)
        x = x + (jax.nn.silu(gate_f) * up) @ w_down[l]
    return x


_drawn_inputs = setup_inputs


def setup_inputs(seed=0):
    import zlib

    import numpy as np

    out = dict(_drawn_inputs(seed))
    spreads = {}
    factors = {'attn_norm': 4.802,
     'a_log': 2.796,
     'gdn_out_norm': 8.0,
     'q_a_norm': 8.0,
     'kv_a_norm': 8.0,
     'q_norm': 8.0,
     'k_norm': 8.0,
     'ffn_norm': 15.135,
     'pool_scale': 3.676}
    for name, (base, spread) in spreads.items():
        noise = np.random.default_rng([zlib.crc32(name.encode()), seed]).standard_normal(out[name].shape)
        drawn = base * np.exp(spread * noise) if base else spread * noise
        out[name] = __import__('jax').numpy.asarray(drawn.astype(out[name].dtype))
    for name, factor in factors.items():
        out[name] = (out[name] * factor).astype(out[name].dtype)
    return out
```

```python
from contextlib import ExitStack

import numpy as np

import concourse.bass as bass
from concourse import mybir

D_MODEL, SEQ, CHUNK = 1024, 1024, 64
GDN_HEADS, GDN_DIM, CONV_WIDTH = 4, 128, 4
POOL_GROUPS, POOL_DIM, POOL_WINDOWS = 4, 64, (2, 4, 8, 16)
HEADS, NOPE, ROPE, V_DIM, Q_RANK, KV_RANK = 4, 64, 32, 64, 256, 128
EPS, ROPE_THETA = 1e-6, 10000.0

P = 128
QK = NOPE + ROPE
HALF = ROPE // 2
OFF_QKV = 0
OFF_GATE = 3 * GDN_HEADS * GDN_DIM
OFF_A = OFF_GATE + GDN_HEADS * GDN_DIM
OFF_POOL = OFF_A + 2 * GDN_HEADS
OFF_CQ = OFF_POOL + POOL_GROUPS * POOL_DIM
OFF_CKV = OFF_CQ + Q_RANK
OFF_KR = OFF_CKV + KV_RANK
FFN_HIDDEN = ((8 * D_MODEL // 3 + 255) // 256) * 256

KT = D_MODEL // P
TT = SEQ // P
BANK = 512
HALVES = SEQ // BANK
QKV_TILES = 3 * GDN_HEADS
GATE_TILES = GDN_HEADS
FIRST_TILES = [OFF_CQ, OFF_CQ + P, OFF_CKV, OFF_POOL, OFF_POOL + P]
IN_TILES = len(FIRST_TILES) + QKV_TILES + GATE_TILES
HID_TILES = FFN_HIDDEN // P
GROUPS = [8, 8, 6]
SMALL = 2 * GDN_HEADS + ROPE
RAW, SPLIT = 4, 2
LEVELS = [1 << s for s in range(7)]
BIG_NEG = -1.0e30
assert sum(GROUPS) == HID_TILES and TT == 8 and HEADS == 4 and GDN_HEADS == 4


class Steps:

    def __init__(self, sem, names, ahead=False):
        self.sem, self.names = sem, list(names)
        self.base = len(self.names) if ahead else 0
        assert len(set(self.names)) == len(self.names)

    def after(self, name, rnd=0):
        return self.base + rnd * len(self.names) + (self.names.index(name) + 1)


def hybrid_block(nc, x, positions, attn_norm, w_in, conv_w, a_log, dt_bias, gdn_out_norm, pool_w, pool_scale,
                 q_a_norm, w_uq, kv_a_norm, w_ukv, q_norm, k_norm, w_out, ffn_norm, w_gate_up, w_down, out):
    f32, f32r, i32 = mybir.dt.float32, mybir.dt.float32r, mybir.dt.int32
    ALU, ACT, AX = mybir.AluOpType, mybir.ActivationFunctionType, mybir.AxisListType
    ds = bass.ds

    class Region:

        def __init__(self, start):
            self.at = start

        def take(self, name, shape, dt=f32):
            t = nc.alloc_sbuf_tensor_at(name, shape, dt, offset=self.at)
            self.at += -(-int(np.prod(shape[1:])) * 4 // 32) * 32
            return t

    SBUF_START, SBUF_END = 16512, 224 * 1024
    c = Region(SBUF_START)
    ident = c.take("ident", [P, P])
    le = c.take("le", [P, P])
    gt = c.take("gt", [P, P])
    ones = c.take("ones", [P, P])
    cols = c.take("cols", [P, 80])
    ab_rows = c.take("ab_rows", [P, 2, GDN_HEADS])
    small_tok = c.take("small_tok", [P, TT, SMALL])
    kr_ss = c.take("kr_ss", [P, TT])
    trig = c.take("trig", [P, 2, TT, HALF])
    g_log = c.take("g_log", [P, TT, GDN_HEADS])
    beta = c.take("beta", [P, TT, GDN_HEADS])
    decays = c.take("decays", [P, 3, TT, GDN_HEADS])
    half_neg = c.take("half_neg", [P, 16])
    half_pos = c.take("half_pos", [P, 16])
    recip_cnt = c.take("recip_cnt", [P, 16])
    ssq = c.take("ssq", [P, TT])
    meansq = c.take("meansq", [P, TT])
    rstd = c.take("rstd", [P, TT])
    tok_sc = [c.take(f"tok_sc{b}", [P, 64]) for b in range(2)]
    row_stat = c.take("row_stat", [P, 4])
    R1 = c.at
    R2 = R1 + 64 * 1024
    R3 = R2 + 64 * 1024

    r = Region(R1)
    act_hi = r.take("act_hi", [P, KT, SEQ], f32r)
    act_lo = r.take("act_lo", [P, KT, SEQ], f32r)
    r = Region(R1)
    oT = r.take("oT", [P, KT, SEQ])
    qT = r.take("qT", [P, HEADS, SEQ])
    kT = r.take("kT", [P, HEADS, SEQ])
    w_out_sb = Region(R1 + 32 * 1024).take("w_out_sb", [P, KT, D_MODEL])
    r = Region(R2)
    qkvT = r.take("qkvT", [P, QKV_TILES, SEQ])
    sgT = r.take("sgT", [P, GATE_TILES, SEQ])
    r = Region(R2)
    hf_hi = r.take("hf_hi", [P, KT, SEQ], f32r)
    hf_lo = r.take("hf_lo", [P, KT, SEQ], f32r)
    r = Region(R3)
    w_hi = [r.take(f"w_hi{s}", [P, KT, P], f32r) for s in range(SPLIT)]
    w_lo = [r.take(f"w_lo{s}", [P, KT, P], f32r) for s in range(SPLIT)]
    raw = [r.take(f"raw{s}", [P, KT, P]) for s in range(RAW)]
    R3_REST = r.at
    cT = r.take("cT", [P, 3, SEQ])
    wuq = r.take("wuq", [P, 2, HEADS * QK])
    wukv = r.take("wukv", [P, HEADS * (NOPE + V_DIM)])
    pw = r.take("pw", [P, 2, P])
    pz = r.take("pz", [P, 2, SEQ])
    stage = [r.take(f"stage{s}", [P, SEQ]) for s in range(2)]
    assert r.at <= SBUF_END, r.at - SBUF_END
    r = Region(R3_REST)
    x2 = r.take("x2", [P, TT, D_MODEL])
    stage2 = [r.take(f"stage2_{s}", [P, SEQ]) for s in range(2)]
    assert r.at <= SBUF_END, r.at - SBUF_END
    x2_sq = Region(R3).take("x2_sq", [P, D_MODEL])
    V = Region(R3_REST + 26 * 1024).take("V", [P, TT, HEADS, V_DIM])
    r = Region(R3_REST + 34 * 1024)
    masks = r.take("masks", [P, len(LEVELS), P])
    qk_gain = Region(r.at).take("qk_gain", [P, 2, QK])
    qh = r.take("qh", [P, SEQ])
    assert r.at <= SBUF_END, r.at - SBUF_END
    r = Region(R3)
    cTf = [r.take(f"cTf{b}", [P, 3, P]) for b in range(2)]
    c_sq = [r.take(f"c_sq{b}", [P, 3, P]) for b in range(2)]
    qk_sq = [r.take(f"qk_sq{b}", [P, HEADS, QK + NOPE]) for b in range(2)]
    qk = [r.take(f"qk{b}", [P, 2, HEADS, QK]) for b in range(2)]
    rot = [r.take(f"rot{b}", [P, 4, 2 * HEADS, HALF]) for b in range(2)]
    assert r.at <= R3_REST
    r = Region(R3)
    qkvf = [r.take(f"qkvf{b}", [P, 12, P]) for b in range(2)]
    E_ = [r.take(f"E{b}", [P, 4, P]) for b in range(2)]
    attn = [r.take(f"attn{b}", [P, 4, P]) for b in range(2)]
    A_ = [r.take(f"A{b}", [P, 4, P]) for b in range(2)]
    B_ = [r.take(f"B{b}", [P, 4, P]) for b in range(2)]
    N_ = [r.take(f"N{b}", [P, 2, 4, P]) for b in range(2)]
    M_ = [r.take(f"M{b}", [P, 4, P]) for b in range(2)]
    kd = [r.take(f"kd{b}", [P, 4, P]) for b in range(2)]
    Vn = [r.take(f"Vn{b}", [P, 4, P]) for b in range(2)]
    S_ = r.take("S", [P, 4, P])
    probs = r.take("probs", [P, SEQ])
    assert r.at <= R3_REST + 26 * 1024, r.at - R3_REST
    probsT = [r.take(f"probsT{g}", [P, 4, P]) for g in range(1)]
    assert r.at <= R3_REST + 26 * 1024 + 0, r.at - R3_REST - 26 * 1024
    rows = qkvT[0:70, 3, 0:P]
    pos_i = nc.alloc_sbuf_tensor_at("pos_i", [P, P], i32, offset=R2 + 4 * SEQ * 4)
    pos_f = qkvT[0:TT, 5, 0:P]
    inv_freq = qkvT[:, 6, 0:HALF]
    ang = qkvT[:, 7, 0:P]
    turns = qkvT[:, 8, 0:P]
    turns_i = nc.alloc_sbuf_tensor_at("turns_i", [P, P], i32, offset=R2 + 9 * SEQ * 4)
    wrap = qkvT[:, 10, 0:2 * P]
    sin_in = qkvT[:, 11, 0:2 * P]
    smallT = qkvT[0:SMALL, 3, :]
    small_raw = sgT[:, 3, 0:KT * SMALL].rearrange("p (k n) -> p k n", k=KT)
    mid = sgT[:, 3, 320:576].rearrange("p (a t h) -> p a t h", a=8, t=TT)
    kr_sq = sgT[:, 3, 576:832].rearrange("p (t n) -> p t n", t=TT)
    assert KT * SMALL <= 320
    x_sq = qkvT[:, 0, :]
    x_scaled = [qkvT[:, 1 + s, :] for s in range(2)]
    C_CONV, C_ATTN, C_FFN, C_QA, C_KVA, C_GDN, C_POOL, C_POS = 0, 48, 56, 64, 66, 67, 68, 70

    ctx = ExitStack()
    with ctx:
        def sem(name):
            return ctx.enter_context(nc.semaphore(name))

        ps = ctx.enter_context(nc.psum_tensor("ps", [P, 8, BANK], f32))

        rows_loaded = sem("rows_loaded")
        x_loaded = [sem(f"raw_loaded{s}") for s in range(RAW)]
        prep_loaded = sem("mla_weights_loaded")
        small_loaded = sem("small_loaded")
        small_turned = sem("small_turned")
        consts_ready = sem("consts_ready")
        pool_chain, dve_chain, act_chain = sem("pool_chain"), sem("dve_chain"), sem("act_chain")
        cols_in_psum = sem("cols_in_psum")
        cols_ready = sem("cols_ready")
        pos_float = sem("pos_float")
        sin_args = sem("sin_args")
        trig_ready = sem("trig_ready")
        x_sumsq = sem("x_sumsq")
        x_rstd = sem("x_rstd")
        raw_used = sem("raw_used")
        x_turned = sem("x_turned")
        bank_pair_free = sem("bank_pair_free")
        gate_pair_free = sem("gate_pair_free")
        stage_read = sem("stage_read")
        h_ready = sem("h_ready")
        hi_split = sem("hi_split")
        gemm_done = sem("gemm_done")

        w_out_loaded = sem("w_out_loaded")
        att_turned = sem("att_turned")
        att_moved = sem("att_moved")
        op_done = sem("out_proj_done")
        x2_ready = sem("x2_ready")
        x2_sumsq, x2_rstd = sem("x2_sumsq"), sem("x2_rstd")
        x2_scaled = sem("x2_scaled")
        x2_turned = sem("x2_turned")
        hf_high, hf_ready = sem("hf_high"), sem("hf_ready")
        silu_done = sem("silu_done")
        hid_mult = sem("hid_mult")
        hid_high, hid_ready = sem("hid_high"), sem("hid_ready")
        y_copied = sem("y_copied")
        y_turned = sem("y_turned")
        x2_added = sem("x2_added")
        stored = sem("stored")
        mla_weights = sem("mla_weights")
        pw_loaded = sem("pw_loaded")
        chunk_loaded = [sem(f"chunk_loaded{b}") for b in range(2)]
        head_loaded = sem("head_loaded")

        mid_pe = Steps(sem("mid_pe"), ["decays", "pool0", "pool1"])
        mid_act = Steps(sem("mid_act"), ["exp_abs", "exp_alog", "exp_b", "ln", "kr_sq", "decays", "pool0", "pool1"])
        mid_dve = Steps(sem("mid_dve"), ["abs", "one_plus", "g"])
        mla_pe = Steps(sem("mla_pe"), ["front0", "front1", "back0", "back1"], ahead=True)
        mla_act = Steps(sem("mla_act"), ["cTf0", "c_sq0", "sq0", "cTf1", "c_sq1", "sq1", "back0", "back1"], ahead=True)
        mla_dve = Steps(sem("mla_dve"), ["latent_ms0", "qk_ms0", "qk0", "latent_ms1", "qk_ms1", "qk1", "kT0", "kT1"],
                        ahead=True)
        mla_pool = Steps(sem("mla_pool"), ["latent_pow0", "qk_pow0", "latent_pow1", "qk_pow1"])
        LINKS_MLA = 10
        LAST = len(LEVELS) - 1
        X_STAGES = [f"x{l}" for l in range(1, LAST + 1)]
        YZ_STAGES = [f"yz{l}" for l in range(1, LAST + 1)]
        levels = [st for pair in zip(X_STAGES, YZ_STAGES) for st in pair]
        GDN_STAGES = ["decay", "kk", "turn", "m0"] + levels + ["ks", "tr", "av", "ot"]
        yz_pe = [n for l in range(1, LAST + 1) for n in ([f"x{l}", f"y{l}"] + ([f"z{l}"] if l < LAST else []))]
        nm_dve = [n for l in range(1, LAST + 1) for n in ([f"n{l}"] + ([f"m{l}"] if l < LAST else []))]
        gp = [Steps(sem(f"gdn_pe{b}"), ["decay", "norms", "kk", "qk", "kT", "vT", "m0"] + yz_pe
                    + ["ks", "qs", "tr", "av", "ds", "ot"], ahead=True) for b in range(2)]
        ga = [Steps(sem(f"gdn_act{b}"), ["sq", "exp", "m0"] + X_STAGES + ["osq"], ahead=True) for b in range(2)]
        gd = [Steps(sem(f"gdn_dve{b}"), ["gtg", "ss", "rc", "c", "et", "att", "a0", "a", "kd", "vn", "rqs", "r2", "n0"]
                    + nm_dve + ["r0", "r", "o1", "v", "s", "o", "osum", "oms0", "oms", "of", "on", "out"], ahead=True)
              for b in range(2)]
        gg = [Steps(sem(f"gdn_pool{b}"), ["rq", "nk", "mask"] + [f"b{l}" for l in range(LAST + 1)] + ["sd", "pow"],
                    ahead=True) for b in range(2)]
        q_tiles = list(range(TT - 1, -1, -1))
        groups_of = {t: (range(2) if t >= 4 else range(1)) for t in q_tiles}
        tp = Steps(sem("att_pe"), [n for t in q_tiles for n in [f"s{t}"] + [f"{w}{t}.{g}" for g in groups_of[t]
                                                                          for w in ("t", "pv")]], ahead=True)
        ta = Steps(sem("att_act"), [n for t in q_tiles for n in [f"e{t}"] + [f"p{t}.{g}" for g in groups_of[t]]],
                   ahead=True)
        td = Steps(sem("att_dve"), [f"{n}{t}" for t in q_tiles for n in ("mask", "rowmax", "max", "rinv", "o")],
                   ahead=True)
        SHIFT = 10
        late = len(GDN_STAGES) - SHIFT
        slot1 = [(st, 1, 1) for st in GDN_STAGES[late:]] + [(st, 1, 0) for st in GDN_STAGES[:late]]
        chunk_part = [e for st, e1 in zip(GDN_STAGES, slot1) for e in ((st, 0, 0), e1)]
        head_part = [e for t in q_tiles for e in [("att_s", t, 0)] + [(w, (t, g), 0) for g in groups_of[t]
                                                                      for w in ("att_t", "att_pv")]]
        ORDER = []
        for n, e in enumerate(chunk_part):
            ORDER += [e] + head_part[n * len(head_part) // len(chunk_part):(n + 1) * len(head_part) // len(chunk_part)]
        FIRST_ROUND = [e for e in ORDER if not e[2]]
        AFTER_ROUNDS = [e for e in ORDER if e[2]]
        U, W = [0, 2], [1, 3]

        def heads_of(m):
            return m[:, :].unsqueeze(1).broadcast_to([P, 4, P])

        def per_head(v):
            return v.unsqueeze(2).broadcast_to([P, 4, P])

        def flat(t):
            return t[:, :, :].rearrange("p h n -> p (h n)")

        def heads_view(bank):
            return bank.rearrange("p (h n) -> p h n", h=4)

        class Chain:

            def __init__(self, eng, sm):
                self.eng, self.sem, self.n, self.extra = eng, sm, 0, 0

            def __call__(self, op):
                op.then_inc(self.sem, 1)
                self.n += 1
                self.eng.wait_ge(self.sem, self.n + self.extra)

            def start_round(self, rnd, per_round):
                self.first, self.per, self.extra = self.n, per_round, rnd * per_round

            def end_rounds(self, count):
                assert self.n - self.first == self.per, (self.n - self.first, self.per)
                self.n = self.first + self.per * count
                self.extra = 0

        def tile_cols(t):
            return ds(t * P, P)

        def proj_col(m):
            return FIRST_TILES[m - 1] if m <= len(FIRST_TILES) else OFF_QKV + (m - 1 - len(FIRST_TILES)) * P

        M_CQ, M_CKV, M_POOL, M_QKV = 1, 3, 4, 1 + len(FIRST_TILES)
        M_GATE = M_QKV + QKV_TILES
        M_SMALL = 2
        IN_ALL = M_GATE + GATE_TILES
        N_X = TT
        N_X2 = N_X + IN_ALL
        F0 = N_X2 + TT
        GEMM_LAG = N_X + TT
        FFN_PLAN = []
        for g in GROUPS:
            n0 = FFN_PLAN[-1][0] + 2 * FFN_PLAN[-1][2] + KT if FFN_PLAN else F0
            FFN_PLAN.append((n0, sum(gr for _, _, gr in FFN_PLAN), g))

        def loaded_count(n):
            return 16 * (n // RAW + 1) - (16 if n % RAW == 0 else 0)

        w_in_v = w_in[0].rearrange("(k p) n -> p k n", p=P)

        block = ctx.enter_context(nc.Block())

        @block.sync
        def _(sp):
            def load_x(t):
                if t >= RAW:
                    sp.wait_ge(raw_used, t - RAW + 1)
                sp.dma_start(raw[t % RAW][:, :, :].rearrange("p k n -> p (k n)"),
                             x[0, t * P:(t + 1) * P, :]).then_inc(x_loaded[t % RAW], 16)

            for t in range(RAW):
                load_x(t)
            sp.dma_start(small_raw[:, :, 0:2 * GDN_HEADS], w_in_v[:, :, OFF_A:OFF_POOL]).then_inc(small_loaded, 16)
            sp.dma_start(small_raw[:, :, 2 * GDN_HEADS:SMALL],
                         w_in_v[:, :, OFF_KR:OFF_KR + ROPE]).then_inc(small_loaded, 16)
            sp.dma_start(ab_rows[:, 0, :], a_log[0].partition_broadcast(P)).then_inc(prep_loaded, 16)
            sp.dma_start(ab_rows[:, 1, :], dt_bias[0].partition_broadcast(P)).then_inc(prep_loaded, 16)
            sp.dma_start(wuq[:, :, :], w_uq[0].rearrange("(k p) n -> p k n", p=P)).then_inc(prep_loaded, 16)
            sp.dma_start(wukv[:, :], w_ukv[0]).then_inc(prep_loaded, 16)
            sp.dma_start(qk_gain[:, 0, :], q_norm[0].partition_broadcast(P)).then_inc(prep_loaded, 16)
            sp.dma_start(qk_gain[:, 1, :], k_norm[0].partition_broadcast(P)).then_inc(prep_loaded, 16)
            for t in range(RAW, TT):
                load_x(t)

            sp.wait_ge(consts_ready, 1)
            for g in range(POOL_GROUPS):
                lo = (g % 2) * POOL_DIM
                sp.dma_start(pw[lo:lo + POOL_DIM, g // 2, lo:lo + POOL_DIM], pool_w[0, g]).then_inc(pw_loaded, 16)

            def load_in_tile(m, s):
                sp.wait_ge(raw_used, N_X + m - RAW + 1)
                sp.dma_start(raw[s][:, :, :], w_in_v[:, :, ds(proj_col(m), P)]).then_inc(x_loaded[s], 16)

            for m in range(1, M_QKV):
                load_in_tile(m, (N_X + m) % RAW)
            with sp.Fori(0, QKV_TILES // 4) as i:
                for b in range(4):
                    load_in_tile(M_QKV + b + i * 4, (N_X + M_QKV + b) % RAW)
            for m in range(M_GATE, IN_ALL):
                load_in_tile(m, (N_X + m) % RAW)

            sp.wait_ge(mla_act.sem, mla_act.after("back1", TT // 2 - 1))
            sp.wait_ge(mla_dve.sem, mla_dve.after("kT1", TT // 2 - 1))
            with sp.Fori(0, TT // 2) as i:
                for b in range(2):
                    sp.wait_ge(gp[b].sem, gp[b].after("qs", i - 1))
                    sp.dma_start(qkvf[b][:, :, :], qkvT[:, :, ds(i * (2 * P) + b * P, P)]).then_inc(chunk_loaded[b], 16)
                    if b == 0:
                        sp.wait_ge(tp.sem, tp.after("s0", i - 1))
                        sp.dma_start(qh[0:QK, :],
                                     qT[0:QK, ds(i, 1), :].rearrange("p a n -> p (a n)")).then_inc(head_loaded, 16)

            sp.wait_ge(tp.sem, tp.after("s0", TT // 2 - 1))
            for k in range(KT):
                sp.dma_start(w_out_sb[:, k, :], w_out[0, k * P:(k + 1) * P, :]).then_inc(w_out_loaded, 16)
            for b in range(2):
                sp.wait_ge(gd[b].sem, gd[b].after("out", TT // 2 - 1))
            sp.wait_ge(td.sem, td.after("o0", TT // 2 - 1))
            for t in range(TT):
                n = N_X2 + t
                if t >= RAW:
                    sp.wait_ge(raw_used, n - RAW + 1)
                sp.dma_start(raw[n % RAW][:, :, :].rearrange("p k n -> p (k n)"),
                             x[0, t * P:(t + 1) * P, :]).then_inc(x_loaded[n % RAW], 16)
            w_gu_v = w_gate_up[0].rearrange("(k p) n -> p k n", p=P)
            w_dn_v = w_down[0].rearrange("(j p) n -> p j n", p=P)
            for gi, (n0, j0, g) in enumerate(FFN_PLAN):
                with sp.Fori(0, g // 2) as i:
                    for b in range(4):
                        sp.wait_ge(raw_used, i * 4 + (n0 + b - RAW + 1))
                        col = (b % 2) * FFN_HIDDEN + (j0 + b // 2) * P
                        sp.dma_start(raw[(n0 + b) % RAW][:, :, :],
                                     w_gu_v[:, :, ds(i * (2 * P) + col, P)]).then_inc(x_loaded[(n0 + b) % RAW], 16)
                n1 = n0 + 2 * g

                def load_down(m, b, count):
                    sp.wait_ge(raw_used, count - RAW + 1)
                    sp.dma_start(raw[(n1 + b) % RAW][:, 0:g, :],
                                 w_dn_v[:, j0:j0 + g, ds(m * P, P)]).then_inc(x_loaded[(n1 + b) % RAW], 16)

                if gi < len(FFN_PLAN) - 1:
                    with sp.Fori(0, KT // 4) as i:
                        for b in range(4):
                            load_down(i * 4 + b, b, i * 4 + (n1 + b))
                else:
                    def store(m):
                        sp.wait_ge(x2_added, gi * KT + m + 1)
                        sp.dma_start(out[0].rearrange("(t p) n -> p t n", p=P)[:, :, m * P:(m + 1) * P],
                                     x2[:, :, m * P:(m + 1) * P]).then_inc(stored, 16)

                    for m in range(KT):
                        load_down(m, m, n1 + m)
                        if m >= RAW:
                            store(m - RAW)
                    for m in range(KT - RAW, KT):
                        store(m)
            sp.wait_ge(stored, 16 * KT)

        @block.gpsimd
        def _(pool):
            link = Chain(pool, pool_chain)
            pool.memset(ones[:, :], 1.0)
            pool.memset(half_neg[:, :], -0.5)
            pool.memset(half_pos[:, :], 0.5)
            pool.memset(pw[:, :, :], 0.0)
            link(pool.memset(ident[:, :], 0.0))
            link(pool.memset(le[:, :], 1.0))
            link(pool.memset(gt[:, :], 1.0))
            pool.affine_select(out=ident[:, :], in_=ident[:, :], compare_op=ALU.not_equal, fill=1.0,
                               base=0, pattern=[[-1, P]], channel_multiplier=1)
            pool.affine_select(out=le[:, :], in_=le[:, :], compare_op=ALU.is_ge, fill=0.0,
                               base=0, pattern=[[1, P]], channel_multiplier=-1)
            pool.affine_select(out=gt[:, :], in_=gt[:, :], compare_op=ALU.is_gt, fill=0.0,
                               base=0, pattern=[[-1, P]], channel_multiplier=1)
            for j in range(16):
                pool.memset(recip_cnt[:, j:j + 1], 1.0 / (j + 1))
            for j in range(HALF):
                last = pool.memset(inv_freq[:, j:j + 1],
                                   float(np.float32(ROPE_THETA) ** np.float32(-2.0 * j / ROPE)))
            last.then_inc(consts_ready, 1)
            for t in range(TT):
                pool.wait_ge(x_sumsq, t + 1)
                link(pool.tensor_scalar(meansq[:, t:t + 1], ssq[:, t:t + 1], 1.0 / D_MODEL, EPS, ALU.mult, ALU.add))
                pool.tensor_tensor(rstd[:, t:t + 1], meansq[:, t:t + 1], half_neg[:, 0:1],
                                   ALU.pow).then_inc(x_rstd, 1)

            for l, s in enumerate(LEVELS):
                blocks = masks[:, l, :].rearrange("p (b u) -> p b u", u=2 * s)
                link(pool.memset(masks[:, l, :], 0.0))
                link(pool.memset(blocks[:, :, s:2 * s], 1.0))
                nb = P // (2 * s)
                link(pool.affine_select(out=blocks, in_=blocks, compare_op=ALU.is_ge, fill=0.0, base=0,
                                        pattern=[[-2 * s, nb], [0, 2 * s]], channel_multiplier=1))
                link(pool.affine_select(out=blocks, in_=blocks, compare_op=ALU.is_ge, fill=0.0, base=s - 1,
                                        pattern=[[2 * s, nb], [0, 2 * s]], channel_multiplier=-1))

            with pool.Fori(0, TT // 2) as i:
                for b in range(2):
                    for name, lo, n in (("latent", 0, 2), ("qk", 16, 8)):
                        pool.wait_ge(mla_dve.sem, mla_dve.after(f"{name}_ms{b}", i))
                        pool.tensor_tensor(tok_sc[b][:, lo + 8:lo + 8 + n], tok_sc[b][:, lo:lo + n],
                                           half_neg[:, 0:n], ALU.pow).then_inc(mla_pool.sem, 1)

            for c_ in gg:
                pool.sem_inc(c_.sem, c_.base)
            def stages(order, rnd):
                for stage_name, b, back in order:
                    i = rnd - back
                    if stage_name == "decay":
                        sc = tok_sc[b]
                        pool.wait_ge(gd[b].sem, gd[b].after("ss", i))
                        pool.tensor_tensor(sc[:, 12:16], sc[:, 0:4], half_neg[:, 0:4], ALU.pow).then_inc(gg[b].sem, 1)
                        pool.tensor_tensor(sc[:, 8:12], sc[:, 4:8], half_pos[:, 0:4], ALU.pow).then_inc(gg[b].sem, 1)
                        pool.wait_ge(ga[b].sem, ga[b].after("exp", i))
                        pool.tensor_tensor(E_[b][:, :, :], E_[b][:, :, :], heads_of(le), ALU.mult).then_inc(gg[b].sem, 1)
                    elif stage_name == "kk":
                        pool.wait_ge(gd[b].sem, gd[b].after("a", i))
                        pool.tensor_tensor(B_[b][:, :, :], A_[b][:, :, :], heads_of(masks[:, 0, :]),
                                           ALU.mult).then_inc(gg[b].sem, 1)
                    elif stage_name == "m0" or stage_name in X_STAGES[:-1]:
                        if stage_name == "m0":
                            l = 1
                            pool.wait_ge(gd[b].sem, gd[b].after("n0", i))
                        else:
                            l = int(stage_name[1:]) + 1
                            pool.wait_ge(gp[b].sem, gp[b].after(stage_name, i))
                        pool.tensor_tensor(B_[b][:, :, :], A_[b][:, :, :], heads_of(masks[:, l, :]),
                                           ALU.mult).then_inc(gg[b].sem, 1)
                    elif stage_name == "ks":
                        pool.wait_ge(gd[b].sem, gd[b].after("et", i))
                        pool.wait_ge(gp[b].sem, gp[b].after("qs", i))
                        pool.tensor_tensor(S_[:, :, :], S_[:, :, :], per_head(tok_sc[b][:, 20:24]),
                                           ALU.mult).then_inc(gg[b].sem, 1)
                    elif stage_name == "ot":
                        sc = tok_sc[b]
                        pool.wait_ge(gd[b].sem, gd[b].after("oms", i))
                        pool.tensor_tensor(sc[:, 32:36], sc[:, 28:32], half_neg[:, 0:4], ALU.pow).then_inc(gg[b].sem, 1)

            stages(FIRST_ROUND, 0)
            with pool.Fori(1, TT // 2) as rnd:
                stages(ORDER, rnd)
            stages(AFTER_ROUNDS, TT // 2)

            for t in range(TT):
                pool.wait_ge(x2_sumsq, t + 1)
                link(pool.tensor_scalar(meansq[:, t:t + 1], ssq[:, t:t + 1], 1.0 / D_MODEL, EPS, ALU.mult, ALU.add))
                pool.tensor_tensor(rstd[:, t:t + 1], meansq[:, t:t + 1], half_neg[:, 0:1],
                                   ALU.pow).then_inc(x2_rstd, 1)

        @block.scalar
        def _(act):
            link = Chain(act, act_chain)
            act.dma_start(rows[0:48, :], conv_w[0].rearrange("j (f p) -> (j f) p", p=P)).then_inc(rows_loaded, 16)
            act.dma_start(rows[48:56, :], attn_norm[0].rearrange("(f p) -> f p", p=P)).then_inc(rows_loaded, 16)
            act.dma_start(rows[56:64, :], ffn_norm[0].rearrange("(f p) -> f p", p=P)).then_inc(rows_loaded, 16)
            act.dma_start(rows[64:66, :], q_a_norm[0].rearrange("(f p) -> f p", p=P)).then_inc(rows_loaded, 16)
            act.dma_start(rows[66:67, :], kv_a_norm[0].rearrange("(f p) -> f p", p=P)).then_inc(rows_loaded, 16)
            act.dma_start(rows[67:68, :], gdn_out_norm[0].rearrange("(f p) -> f p", p=P)).then_inc(rows_loaded, 16)
            act.dma_start(rows[68:70, :], pool_scale[0].rearrange("(f p) -> f p", p=P)).then_inc(rows_loaded, 16)
            act.dma_start(pos_i[0:TT, :], positions[0].rearrange("(f p) -> f p", p=P)).then_inc(rows_loaded, 16)

            def x_square(t):
                act.wait_ge(x_loaded[t % RAW], 16 * (t // RAW + 1))
                if t >= 1:
                    act.wait_ge(x_sumsq, t)
                act.activation(x_sq, raw[t % RAW][:, :, :].rearrange("p k n -> p (k n)"), ACT.Square,
                               accum_out=ssq[:, t:t + 1]).then_inc(x_sumsq, 1)

            AHEAD = 3
            for t in range(AHEAD):
                x_square(t)
            for t in range(TT):
                if t + AHEAD < TT:
                    x_square(t + AHEAD)
                act.wait_ge(bank_pair_free, t + 1)
                act.activation(act_hi[:, :, tile_cols(t)], stage[t % 2][:, :].rearrange("p (k n) -> p k n", k=KT),
                               ACT.Copy).then_inc(stage_read, 1)
            def split_hi(m, slot, rawslot, rnd):
                act.wait_ge(x_loaded[rawslot], rnd)
                act.activation(w_hi[slot][:, :, :], raw[rawslot][:, :, :], ACT.Copy).then_inc(hi_split, 1)

            def in_round(m):
                return loaded_count(N_X + m)

            act.wait_ge(small_loaded, 2 * 16)
            act.activation(w_hi[0][:, :, 0:SMALL], small_raw, ACT.Copy).then_inc(hi_split, 1)
            split_hi(1, 1, 1, in_round(1))
            act.wait_ge(sin_args, 1)
            act.activation(trig[:, :, :, :].rearrange("p a t f -> p (a t f)"), sin_in, ACT.Sin).then_inc(trig_ready, 1)

            for m in range(M_QKV):
                act.wait_ge(gemm_done, m + 1)
                split_hi(m + 2, m % 2, (N_X + m + 2) % RAW, in_round(m + 2))
                if m == M_SMALL:
                    act.wait_ge(mid_dve.sem, mid_dve.after("abs"))
                    act.activation(mid[:, 2, :, :], mid[:, 1, :, :], ACT.Exp, scale=-1.0).then_inc(mid_act.sem, 1)
                    act.activation(mid[:, 5, 0, :], ab_rows[:, 0, :], ACT.Exp).then_inc(mid_act.sem, 1)
                    act.activation(mid[:, 6, :, :], small_tok[:, :, GDN_HEADS:2 * GDN_HEADS], ACT.Exp,
                                   scale=-1.0).then_inc(mid_act.sem, 1)
                    act.wait_ge(mid_dve.sem, mid_dve.after("one_plus"))
                    act.activation(mid[:, 3, :, :], mid[:, 3, :, :], ACT.Ln).then_inc(mid_act.sem, 1)
                    act.activation(kr_sq, small_tok[:, :, 2 * GDN_HEADS:SMALL], ACT.Square).then_inc(mid_act.sem, 1)
                if m == M_SMALL + 2:
                    act.wait_ge(mid_pe.sem, mid_pe.after("decays"))
                    act.activation(decays[:, :, :, :].rearrange("p a t h -> p (a t h)"),
                                   ps[:, 6, 0:3 * TT * GDN_HEADS], ACT.Exp).then_inc(mid_act.sem, 1)

            def silu_qkv(f, s):
                act.wait_ge(bank_pair_free, f + (TT + M_QKV + 1))
                act.activation(qkvT[:, ds(f, 1), :].rearrange("p a n -> p (a n)"), stage[s][:, :],
                               ACT.Silu).then_inc(stage_read, 1)

            with act.Fori(0, QKV_TILES // 4) as i:
                for b in range(4):
                    m = M_QKV + b
                    act.wait_ge(gemm_done, i * 4 + (m + 1))
                    split_hi(None, m % 2, (N_X + m + 2) % RAW, in_round(m + 2) + i * 16)
                    silu_qkv(b + i * 4, m % 2)
            for m in range(M_GATE, IN_ALL):
                act.wait_ge(gemm_done, m + 1)
                if m + 2 < IN_ALL:
                    split_hi(m + 2, m % 2, (N_X + m + 2) % RAW, in_round(m + 2))
                pair = (m % 2) * 2
                act.activation(sgT[:, m - M_GATE, :], ps[:, pair:pair + 2, :].rearrange("p a n -> p (a n)"),
                               ACT.Silu).then_inc(gate_pair_free, 1)

            for p in range(2):
                act.wait_ge(mid_pe.sem, mid_pe.after(f"pool{p}"))
                act.activation(oT[:, 4 + p, :], ps[:, 4 + 2 * p:6 + 2 * p, :].rearrange("p a n -> p (a n)"), ACT.Copy,
                               scale=cols[:, C_POOL + p:C_POOL + p + 1]).then_inc(mid_act.sem, 1)

            act.sem_inc(mla_act.sem, mla_act.base)
            with act.Fori(0, TT // 2) as i:
                for b in range(2):
                    tile = ds(i * (2 * P) + b * P, P)
                    act.wait_ge(mla_pe.sem, mla_pe.after(f"back{b}", i - 1))
                    act.activation(cTf[b][:, :, :], cT[:, :, tile], ACT.Copy).then_inc(mla_act.sem, 1)
                    act.activation(c_sq[b][:, :, :], cT[:, :, tile], ACT.Square).then_inc(mla_act.sem, 1)
                    act.wait_ge(mla_dve.sem, mla_dve.after(f"kT{b}", i - 1))
                    act.wait_ge(mla_pe.sem, mla_pe.after(f"front{b}", i))
                    act.activation(qk_sq[b][:, :, 0:QK], ps[:, 4 * b + 1, 0:HEADS * QK].rearrange(
                        "p (h d) -> p h d", h=HEADS), ACT.Square)
                    act.activation(qk_sq[b][:, :, QK:QK + NOPE], ps[:, 4 * b + 2, :].rearrange(
                        "p (h d) -> p h d", h=HEADS)[:, :, 0:NOPE], ACT.Square).then_inc(mla_act.sem, 1)
                for b in range(2):
                    act.wait_ge(mla_pe.sem, mla_pe.after(f"back{b}", i))
                    act.activation(qT[0:QK, :, ds(i * (2 * P) + b * P, P)], ps[0:QK, 4 * b + 3, :].rearrange(
                        "p (h d) -> p h d", h=HEADS), ACT.Copy).then_inc(mla_act.sem, 1)

            act.sem_inc(ga[0].sem, len(ga[0].names))
            act.sem_inc(ga[1].sem, len(ga[1].names))
            act.sem_inc(ta.sem, len(ta.names))
            act.wait_ge(mla_dve.sem, mla_dve.after("kT1", TT // 2 - 1))
            def stages(order, rnd):
                def gsig(b, ins):
                    ins.then_inc(ga[b].sem, 1)

                def gafter(c, name, rnd=None):
                    act.wait_ge(c.sem, c.after(name, i if rnd is None else rnd))

                for stage_name, b, back in order:
                    i = rnd - back
                    if stage_name == "decay":
                        act.wait_ge(chunk_loaded[b], i * 16 + 16)
                        gafter(gp[b], "ot", i - 1)
                        gsig(b, act.activation(N_[b][:, :, :, :].rearrange("p a h n -> p (a h) n"),
                                               qkvf[b][:, 0:8, :], ACT.Square))
                        gafter(gp[b], "decay")
                        gsig(b, act.activation(flat(E_[b]), ps[:, U[b], :], ACT.Exp))
                    elif stage_name == "m0":
                        gafter(gp[b], "m0")
                        gsig(b, act.activation(flat(M_[b]), ps[:, W[b], :], ACT.Copy))
                    elif stage_name in X_STAGES:
                        gafter(gp[b], stage_name)
                        gsig(b, act.activation(qkvf[b][:, 8:12, :].rearrange("p h n -> p (h n)"), ps[:, U[b], :],
                                               ACT.Copy))
                    elif stage_name == "av":
                        gafter(gd[b], "o")
                        gsig(b, act.activation(flat(Vn[b]), flat(M_[b]), ACT.Square))
                    elif stage_name == "att_s":
                        w = (b + 1) * P
                        gafter(td, f"max{b}")
                        if b < TT - 1:
                            gafter(tp, f"t{b + 1}.{b + 1 >= 4:d}")
                        else:
                            gafter(tp, "t0.0", i - 1)
                        act.activation(probs[:, 0:w], ps[:, 4:6, :].rearrange("p a n -> p (a n)")[:, 0:w], ACT.Exp,
                                       bias=row_stat[:, 0:1], accum_out=row_stat[:, 1:2]).then_inc(ta.sem, 1)
                    elif stage_name == "att_t":
                        t, g = b
                        n = min(4, t + 1 - 4 * g) * P
                        gafter(tp, f"t{t}.{g}")
                        act.activation(flat(probsT[0])[:, 0:n], ps[:, 6, 0:n], ACT.Copy).then_inc(ta.sem, 1)

            stages(FIRST_ROUND, 0)
            with act.Fori(1, TT // 2) as rnd:
                stages(ORDER, rnd)
            stages(AFTER_ROUNDS, TT // 2)

            for q4 in range(4):
                act.wait_ge(att_turned, q4 + 1)
                act.activation(oT[:, 6:8, q4 * 2 * P:(q4 + 1) * 2 * P],
                               ps[:, 4 + q4, :].rearrange("p (j n) -> p j n", j=2), ACT.Copy).then_inc(att_moved, 1)

            def x2_high(t):
                act.wait_ge(raw_used, N_X2 + t + 1)
                act.activation(hf_hi[:, :, tile_cols(t)], stage2[t % 2][:, :].rearrange("p (k n) -> p k n", k=KT),
                               ACT.Copy).then_inc(hf_high, 1)

            for t in range(TT):
                s = (N_X2 + t) % RAW
                act.wait_ge(x2_ready, t + 1)
                if t >= 1:
                    act.wait_ge(x2_sumsq, t)
                act.activation(x2_sq[:, :], x2[:, t, :], ACT.Square, accum_out=ssq[:, t:t + 1]).then_inc(x2_sumsq, 1)
                act.wait_ge(x2_rstd, t + 1)
                act.activation(raw[s][:, :, :].rearrange("p k n -> p (k n)"), x2[:, t, :], ACT.Copy,
                               scale=rstd[:, t:t + 1]).then_inc(x2_scaled, 1)
                if t >= 1:
                    x2_high(t - 1)
            x2_high(TT - 1)

            def ffn_split_hi(n, count):
                act.wait_ge(x_loaded[n % RAW], count)
                act.activation(w_hi[n % 2][:, :, :], raw[n % RAW][:, :, :], ACT.Copy).then_inc(hi_split, 1)

            for n in (F0, F0 + 1):
                ffn_split_hi(n, loaded_count(n))
            for gi, (n0, j0, g) in enumerate(FFN_PLAN):
                with act.Fori(0, g // 2) as i:
                    for b in range(4):
                        n, s = n0 + b, b // 2
                        act.wait_ge(gemm_done, i * 4 + (n + 1 - GEMM_LAG))
                        ffn_split_hi(n + 2, loaded_count(n + 2) + i * 16)
                        if b % 2 == 0:
                            act.wait_ge(hid_ready, i * 2 + (j0 + s))
                            act.activation(stage2[s][:, :], ps[:, 0:2, :].rearrange("p a n -> p (a n)"),
                                           ACT.Silu).then_inc(silu_done, 1)
                        else:
                            act.wait_ge(hid_mult, i * 2 + (j0 + s + 1))
                            act.activation(act_hi[:, ds(i * 2 + s, 1), :].rearrange("p a n -> p (a n)"),
                                           stage2[s][:, :], ACT.Copy).then_inc(hid_high, 1)

                def down_item(b, rnd, split):
                    n = n0 + 2 * g + b
                    act.wait_ge(gemm_done, rnd * 4 + (n + 1 - GEMM_LAG))
                    if split:
                        ffn_split_hi(n + 2, loaded_count(n + 2) + rnd * 16)
                    if gi > 0 or b >= 2:
                        act.wait_ge(y_turned, rnd * 4 + (gi * KT + b - 1))
                    elif not isinstance(rnd, int):
                        act.wait_ge(y_turned, rnd * 4 + 0)
                    act.activation(stage2[b % 2][:, :], ps[:, 4 + (b % 2) * 2:6 + (b % 2) * 2, :].rearrange(
                        "p a n -> p (a n)"), ACT.Copy).then_inc(y_copied, 1)

                if gi < len(FFN_PLAN) - 1:
                    with act.Fori(0, KT // 4) as i:
                        for b in range(4):
                            down_item(b, i, True)
                else:
                    for m in range(KT):
                        down_item(m, 0, m + 2 < KT)

        @block.vector
        def _(dve):
            link = Chain(dve, dve_chain)

            dve.wait_ge(rows_loaded, 8 * 16)
            dve.tensor_copy(pos_f, pos_i[0:TT, :]).then_inc(pos_float, 1)
            dve.wait_ge(cols_in_psum, 1)
            link(dve.tensor_copy(cols[:, 0:C_POS + TT], ps[:, 7, 0:C_POS + TT]))

            def x_scale(t):
                dve.wait_ge(x_rstd, t + 1)
                if t >= 2:
                    dve.wait_ge(x_turned, t - 1)
                dve.tensor_scalar(x_scaled[t % 2], raw[t % RAW][:, :, :].rearrange("p k n -> p (k n)"),
                                  rstd[:, t:t + 1], None, ALU.mult).then_inc(raw_used, 1)

            def x_gain(t):
                dve.wait_ge(x_turned, t + 1)
                if t >= 2:
                    dve.wait_ge(h_ready, t - 1)
                pair = (t % 2) * 2
                dve.tensor_tensor(stage[t % 2][:, :].rearrange("p (k n) -> p k n", k=KT),
                                  ps[:, pair:pair + 2, :].rearrange("p a (k n) -> p (a k) n", n=P),
                                  cols[:, C_ATTN:C_ATTN + KT].unsqueeze(2).broadcast_to([P, KT, P]),
                                  ALU.mult).then_inc(bank_pair_free, 1)

            def x_low(t):
                dve.wait_ge(stage_read, t + 1)
                dve.tensor_tensor(act_lo[:, :, tile_cols(t)], stage[t % 2][:, :].rearrange("p (k n) -> p k n", k=KT),
                                  act_hi[:, :, tile_cols(t)].bitcast(f32), ALU.subtract).then_inc(h_ready, 1)

            x_scale(0)
            for t in range(TT):
                if t + 1 < TT:
                    x_scale(t + 1)
                if t >= 1:
                    x_low(t - 1)
                x_gain(t)
            x_low(TT - 1)

            def split_lo(m, slot, rawslot):
                dve.wait_ge(hi_split, m + 1)
                dve.tensor_tensor(w_lo[slot][:, :, :], raw[rawslot][:, :, :], w_hi[slot][:, :, :].bitcast(f32),
                                  ALU.subtract).then_inc(raw_used, 1)

            def sig(c, ins):
                ins.then_inc(c.sem, 1)

            def mid_after(c, name):
                dve.wait_ge(c.sem, c.after(name))

            def decays_and_betas():
                dve.wait_ge(prep_loaded, 6 * 16)
                dve.wait_ge(small_turned, 1)
                link(dve.tensor_copy(small_tok[:, :, :].rearrange("p t n -> p (t n)"), ps[:, 6, 0:TT * SMALL]))
                link(dve.tensor_tensor(mid[:, 0, :, :], small_tok[:, :, 0:GDN_HEADS],
                                       ab_rows[:, 1, :].unsqueeze(1).broadcast_to([P, TT, GDN_HEADS]), ALU.add))
                sig(mid_dve, dve.scalar_tensor_tensor(mid[:, 1, :, :], mid[:, 0, :, :], -1.0, mid[:, 0, :, :],
                                                      ALU.mult, ALU.max))
                for k in range(2):
                    dve.tensor_scalar(wuq[:, k, :], wuq[:, k, :], cols[:, C_QA + k:C_QA + k + 1], None, ALU.mult)
                dve.tensor_scalar(wukv[:, :], wukv[:, :], cols[:, C_KVA:C_KVA + 1], None,
                                  ALU.mult).then_inc(mla_weights, 1)
                mid_after(mid_act, "exp_abs")
                sig(mid_dve, dve.tensor_scalar(mid[:, 3, :, :], mid[:, 2, :, :], 1.0, None, ALU.add))
                mid_after(mid_act, "exp_b")
                link(dve.tensor_scalar(mid[:, 7, :, :], mid[:, 6, :, :], 1.0, None, ALU.add))
                link(dve.reciprocal(beta[:, :, :], mid[:, 7, :, :]))
                mid_after(mid_act, "ln")
                link(dve.scalar_tensor_tensor(mid[:, 4, :, :], mid[:, 0, :, :], 0.0, mid[:, 3, :, :], ALU.max, ALU.add))
                sig(mid_dve, dve.scalar_tensor_tensor(g_log[:, :, :], mid[:, 4, :, :], -1.0,
                                                      mid[:, 5, 0, :].unsqueeze(1).broadcast_to([P, TT, GDN_HEADS]),
                                                      ALU.mult, ALU.mult))
                mid_after(mid_act, "kr_sq")
                link(dve.tensor_reduce(kr_ss[:, :], kr_sq, axis=AX.X, op=ALU.add))

            def pair_of(m):
                return ps[:, (m % 2) * 2:(m % 2) * 2 + 2, :].rearrange("p a n -> p (a n)")

            dve.wait_ge(hi_split, 1)
            dve.tensor_tensor(w_lo[0][:, :, 0:SMALL], small_raw, w_hi[0][:, :, 0:SMALL].bitcast(f32),
                              ALU.subtract).then_inc(raw_used, 1)
            split_lo(1, 1, 1)
            ang_v = ang.rearrange("p (t f) -> p t f", t=TT)
            link(dve.tensor_tensor(ang_v, cols[:, C_POS:C_POS + TT].unsqueeze(2).broadcast_to([P, TT, HALF]),
                                   inv_freq.unsqueeze(1).broadcast_to([P, TT, HALF]), ALU.mult))
            two_pi = 2.0 * np.pi
            c1 = 6.28125
            c2 = float(np.float32(np.floor((two_pi - c1) * 2.0 ** 20) / 2.0 ** 20))
            c3 = two_pi - c1 - c2
            link(dve.tensor_scalar(turns, ang, 1.0 / two_pi, None, ALU.mult))
            link(dve.tensor_copy(turns_i[:, :], turns))
            link(dve.tensor_copy(turns, turns_i[:, :]))
            for part in (c1, c2, c3):
                link(dve.scalar_tensor_tensor(ang, turns, -part, ang, ALU.mult, ALU.add))
            link(dve.tensor_copy(sin_in[:, P:2 * P], ang))
            link(dve.tensor_scalar(sin_in[:, 0:P], ang, np.pi / 2, None, ALU.add))
            for bound, op, shift in ((np.pi, ALU.is_gt, -two_pi), (-np.pi, ALU.is_lt, two_pi)):
                link(dve.tensor_scalar(wrap, sin_in, bound, shift, op, ALU.mult))
                link(dve.tensor_tensor(sin_in, sin_in, wrap, ALU.add))
            dve.tensor_scalar(sin_in, sin_in, 3.1415925, -3.1415925, ALU.min, ALU.max).then_inc(sin_args, 1)

            for m in range(M_QKV):
                dve.wait_ge(gemm_done, m + 1)
                split_lo(m + 2, m % 2, (N_X + m + 2) % RAW)
                if m == 0:
                    dve.tensor_copy(smallT, ps[0:SMALL, 0:2, :].rearrange("p a n -> p (a n)")).then_inc(
                        bank_pair_free, 1)
                elif m < M_POOL:
                    dve.tensor_copy(cT[:, m - 1, :], pair_of(m)).then_inc(bank_pair_free, 1)
                    if m == M_SMALL:
                        decays_and_betas()
                else:
                    p = m - M_POOL
                    px, sums = sgT[:, 0, :], [sgT[:, 1, :], sgT[:, 2, :]]
                    dve.tensor_copy(px, pair_of(m)).then_inc(bank_pair_free, 1)
                    dve.wait_ge(bank_pair_free, TT + m + 1)
                    src, width, n = px, 1, 0
                    lows = {}
                    while width < POOL_WINDOWS[2 * p + 1]:
                        r0 = 64 if 2 * width > POOL_WINDOWS[2 * p] else 0
                        dst = sums[n % 2]
                        dve.tensor_copy(dst[r0:P, 0:width], src[r0:P, 0:width])
                        link(dve.tensor_tensor(dst[r0:P, width:SEQ], src[r0:P, width:SEQ], src[r0:P, 0:SEQ - width],
                                               ALU.add))
                        width *= 2
                        lows[width] = dst
                        src, n = dst, n + 1
                    for g in range(2):
                        w = POOL_WINDOWS[2 * p + g]
                        rr = slice(64 * g, 64 * g + 64)
                        s_w = lows[w]
                        dve.scalar_tensor_tensor(pz[rr, p, w - 1:SEQ], s_w[rr, w - 1:SEQ], 1.0 / w, px[rr, w - 1:SEQ],
                                                 ALU.mult, ALU.subtract)
                        link(dve.tensor_tensor(pz[rr, p, 0:w - 1], s_w[rr, 0:w - 1], recip_cnt[rr, 0:w - 1], ALU.mult))
                        link(dve.tensor_tensor(pz[rr, p, 0:w - 1], pz[rr, p, 0:w - 1], px[rr, 0:w - 1], ALU.subtract))

            with dve.Fori(0, QKV_TILES // 4) as i:
                link.start_round(i, 3 * 4)
                for b in range(4):
                    m, s = M_QKV + b, (M_QKV + b) % 2
                    dve.wait_ge(gemm_done, i * 4 + (m + 1))
                    split_lo(m + 2 + i * 4, s, (N_X + m + 2) % RAW)
                    dve.wait_ge(stage_read, i * 4 + (TT + b - 1))
                    src, dst = pair_of(m), stage[s]

                    def tap(j):
                        return cols[:, ds(C_CONV + j * QKV_TILES + b + i * 4, 1)]

                    link(dve.tensor_scalar(dst[:, :], src, tap(3), None, ALU.mult))
                    for d in (1, 2, 3):
                        op = dve.scalar_tensor_tensor(dst[:, d:SEQ], src[:, 0:SEQ - d], tap(3 - d), dst[:, d:SEQ],
                                                      ALU.mult, ALU.add)
                        if d < 3:
                            link(op)
                    op.then_inc(bank_pair_free, 1)
            link.end_rounds(QKV_TILES // 4)
            for m in range(M_GATE, IN_ALL - 2):
                split_lo(m + 2, m % 2, (N_X + m + 2) % RAW)

            dve.wait_ge(gemm_done, IN_ALL)
            dve.wait_ge(stage_read, TT + QKV_TILES)
            dve.sem_inc(mla_dve.sem, mla_dve.base)
            with dve.Fori(0, TT // 2) as i:
                def mafter(c, name, rnd=None):
                    dve.wait_ge(c.sem, c.after(name, i if rnd is None else rnd))

                for b in range(2):
                    t = i * 2 + b
                    sc = tok_sc[b]
                    bank = 4 * b
                    if b == 0:
                        link.start_round(i, 2 * LINKS_MLA)
                    n0 = link.n
                    mafter(mla_act, f"sq{b}")
                    link(dve.tensor_copy(sc[:, 2:5], ps[:, bank, 0:3]))
                    link(dve.tensor_tensor(sc[:, 5:6], sc[:, 2:3], sc[:, 3:4], ALU.add))
                    link(dve.tensor_scalar(sc[:, 0:1], sc[:, 5:6], 1.0 / Q_RANK, EPS, ALU.mult, ALU.add))
                    sig(mla_dve, dve.tensor_scalar(sc[:, 1:2], sc[:, 4:5], 1.0 / KV_RANK, EPS, ALU.mult, ALU.add))
                    mafter(mla_dve, f"latent_ms{b}")
                    dve.tensor_reduce(sc[:, 32:36], qk_sq[b][:, :, 0:QK], axis=AX.X, op=ALU.add)
                    link(dve.tensor_reduce(sc[:, 36:40], qk_sq[b][:, :, QK:QK + NOPE], axis=AX.X, op=ALU.add))
                    link(dve.reciprocal(sc[:, 10:12], sc[:, 0:2]))
                    dve.tensor_scalar(sc[:, 40:44], sc[:, 32:36], sc[:, 10:11], None, ALU.mult)
                    link(dve.tensor_scalar(sc[:, 44:48], sc[:, 36:40], sc[:, 11:12], kr_ss[:, ds(t, 1)],
                                           ALU.mult, ALU.add))
                    sig(mla_dve, dve.tensor_scalar(sc[:, 16:24], sc[:, 40:48], 1.0 / QK, EPS, ALU.mult, ALU.add))
                    dve.wait_ge(mla_pool.sem, mla_pool.after(f"qk_pow{b}", i))
                    dve.tensor_scalar(sc[:, 48:52], sc[:, 24:28], sc[:, 8:9], float(QK) ** -0.5, ALU.mult, ALU.mult)
                    dve.tensor_scalar(V[:, ds(t, 1), :, :].rearrange("p a h d -> p (a h) d"),
                                      ps[:, bank + 2, :].rearrange("p (h d) -> p h d", h=HEADS)[:, :, NOPE:],
                                      sc[:, 9:10], None, ALU.mult)
                    link(dve.tensor_scalar(sc[:, 52:56], sc[:, 28:32], sc[:, 9:10], None, ALU.mult))
                    mafter(mla_pe, f"back{b}", i - 1)
                    q_, k_ = qk[b][:, 0, :, :], qk[b][:, 1, :, :]
                    dve.tensor_tensor(q_, ps[:, bank + 1, 0:HEADS * QK].rearrange("p (h d) -> p h d", h=HEADS),
                                      sc[:, 48:52].unsqueeze(2).broadcast_to([P, HEADS, QK]), ALU.mult)
                    dve.tensor_tensor(k_[:, :, 0:NOPE],
                                      ps[:, bank + 2, :].rearrange("p (h d) -> p h d", h=HEADS)[:, :, 0:NOPE],
                                      sc[:, 52:56].unsqueeze(2).broadcast_to([P, HEADS, NOPE]), ALU.mult)
                    link(dve.tensor_tensor(k_[:, :, NOPE:QK],
                                           small_tok[:, ds(t, 1), 2 * GDN_HEADS:SMALL].broadcast_to([P, HEADS, ROPE]),
                                           sc[:, 28:32].unsqueeze(2).broadcast_to([P, HEADS, ROPE]), ALU.mult))
                    link(dve.tensor_tensor(qk[b][:, :, :, :], qk[b][:, :, :, :],
                                           qk_gain[:, :, :].unsqueeze(2).broadcast_to([P, 2, HEADS, QK]), ALU.mult))
                    both = qk[b][:, :, :, :].rearrange("p a h d -> p (a h) d")
                    x1, x2_ = both[:, :, NOPE:NOPE + HALF], both[:, :, NOPE + HALF:QK]
                    cos = trig[:, 0, ds(t, 1), :].broadcast_to([P, 2 * HEADS, HALF])
                    sin = trig[:, 1, ds(t, 1), :].broadcast_to([P, 2 * HEADS, HALF])
                    ro = rot[b]
                    dve.tensor_tensor(ro[:, 0, :, :], x1, cos, ALU.mult)
                    dve.tensor_tensor(ro[:, 1, :, :], x2_, sin, ALU.mult)
                    dve.tensor_tensor(ro[:, 2, :, :], x2_, cos, ALU.mult)
                    link(dve.tensor_tensor(ro[:, 3, :, :], x1, sin, ALU.mult))
                    dve.tensor_tensor(x1, ro[:, 0, :, :], ro[:, 1, :, :], ALU.subtract)
                    sig(mla_dve, dve.tensor_tensor(x2_, ro[:, 2, :, :], ro[:, 3, :, :], ALU.add))
                    assert link.n - n0 == LINKS_MLA, link.n - n0
                for b in range(2):
                    mafter(mla_pe, f"back{b}")
                    sig(mla_dve, dve.tensor_copy(kT[0:QK, :, ds(i * (2 * P) + b * P, P)],
                                                 ps[0:QK, 4 * b, :].rearrange("p (h d) -> p h d", h=HEADS)))
            link.end_rounds(TT // 2)

            for c_ in (gd[0], gd[1], td):
                dve.sem_inc(c_.sem, len(c_.names))
            dve.wait_ge(mla_act.sem, mla_act.after("back1", TT // 2 - 1))
            link(dve.memset(S_[:, :, :], 0.0))
            def stages(order, rnd):
                def gafter(c, name, rnd=None):
                    dve.wait_ge(c.sem, c.after(name, i if rnd is None else rnd))

                def decay(which, b):
                    return decays[:, which, ds(i * 2 + b, 1), :].rearrange("p a h -> p (a h)")

                for stage_name, b, back in order:
                    i = rnd - back
                    if stage_name in GDN_STAGES:
                        sc, bank_u, bank_w = tok_sc[b], heads_view(ps[:, U[b], :]), heads_view(ps[:, W[b], :])
                        e, a, bm, m_, n_ = E_[b], A_[b], B_[b], M_[b], N_[b]

                        def own(name, rnd=None):
                            gafter(gd[b], name, rnd)

                        def gsig(ins):
                            sig(gd[b], ins)
                    if stage_name == "decay":
                        own("out", i - 1)
                        gsig(dve.tensor_tensor(bm[:, :, :], heads_of(gt),
                                               per_head(g_log[:, ds(i * 2 + b, 1), :].rearrange("p a h -> p (a h)")),
                                               ALU.mult))
                        gafter(gp[b], "norms")
                        gsig(dve.tensor_scalar(sc[:, 0:8], ps[:, W[b], 0:8], EPS, None, ALU.add))
                        own("ss")
                        gsig(dve.reciprocal(sc[:, 24:28], sc[:, 4:8]))
                        own("rc")
                        gsig(dve.tensor_tensor(sc[:, 16:20], sc[:, 24:28],
                                               beta[:, ds(i * 2 + b, 1), :].rearrange("p a h -> p (a h)"), ALU.mult))
                        gafter(gg[b], "sd", i - 1)
                        gsig(dve.tensor_copy(sc[:, 20:24], decay(2, b)))
                    elif stage_name == "kk":
                        gafter(gg[b], "mask")
                        gafter(gp[b], "qk")
                        own("c")
                        gsig(dve.tensor_tensor(attn[b][:, :, :], bank_w, e[:, :, :], ALU.mult))
                        gsig(dve.tensor_tensor(a[:, :, :], bank_u, e[:, :, :], ALU.mult))
                        own("a0")
                        gsig(dve.tensor_tensor(a[:, :, :], a[:, :, :], per_head(sc[:, 16:20]), ALU.mult))
                    elif stage_name == "turn":
                        gafter(gp[b], "vT")
                        gsig(dve.tensor_tensor(kd[b][:, :, :], bank_w, per_head(decay(1, b)), ALU.mult))
                        gafter(gg[b], "nk")
                        gsig(dve.tensor_tensor(Vn[b][:, :, :], bank_u, per_head(sc[:, 8:12]), ALU.mult))
                        gsig(dve.tensor_scalar(sc[:, 12:16], sc[:, 12:16], float(GDN_DIM) ** -0.5, None, ALU.mult))
                        own("rqs")
                        gsig(dve.tensor_tensor(sc[:, 36:40], sc[:, 12:16], sc[:, 12:16], ALU.mult))
                    elif stage_name == "m0":
                        gafter(gg[b], "b0")
                        gafter(gp[b], "norms")
                        gsig(dve.tensor_tensor(n_[:, 0, :, :], heads_of(ident), bm[:, :, :], ALU.subtract))
                    elif stage_name in YZ_STAGES:
                        l = int(stage_name[2:])
                        gafter(gp[b], f"y{l}")
                        gsig(dve.tensor_tensor(n_[:, l % 2, :, :], n_[:, (l - 1) % 2, :, :], bank_w, ALU.subtract))
                        if l < LAST:
                            gafter(gp[b], f"z{l}")
                            gsig(dve.tensor_tensor(m_[:, :, :], m_[:, :, :], bank_u, ALU.subtract))
                    elif stage_name == "ks":
                        gafter(gp[b], "ks")
                        gsig(dve.tensor_tensor(e[:, :, :], bank_u, per_head(decay(0, b)), ALU.mult))
                        own("r0")
                        gsig(dve.tensor_tensor(e[:, :, :], Vn[b][:, :, :], e[:, :, :], ALU.subtract))
                        gafter(gp[b], "qs")
                        gsig(dve.tensor_tensor(bm[:, :, :], bank_w, per_head(decay(0, b)), ALU.mult))
                    elif stage_name == "tr":
                        gafter(gp[b], "tr")
                        gsig(dve.tensor_tensor(a[:, :, :], bank_u, per_head(sc[:, 16:20]), ALU.mult))
                    elif stage_name == "av":
                        gafter(gp[b], "ds")
                        gafter(gg[b], "sd")
                        gsig(dve.tensor_tensor(S_[:, :, :], S_[:, :, :], bank_w, ALU.add))
                        own("o1")
                        gsig(dve.tensor_tensor(m_[:, :, :], bm[:, :, :], bank_u, ALU.add))
                    elif stage_name == "ot":
                        gafter(ga[b], "osq")
                        gsig(dve.tensor_reduce(sc[:, 24:28], Vn[b][:, :, :], axis=AX.X, op=ALU.add))
                        own("osum")
                        gsig(dve.scalar_tensor_tensor(sc[:, 28:32], sc[:, 24:28], 1.0 / GDN_DIM, sc[:, 36:40],
                                                      ALU.mult, ALU.mult))
                        own("oms0")
                        gsig(dve.tensor_scalar(sc[:, 28:32], sc[:, 28:32], EPS, None, ALU.add))
                        gafter(gg[b], "pow")
                        gsig(dve.tensor_tensor(sc[:, 40:44], sc[:, 32:36], sc[:, 12:16], ALU.mult))
                        own("of")
                        gsig(dve.tensor_tensor(n_[:, 1, :, :], m_[:, :, :], per_head(sc[:, 40:44]), ALU.mult))
                        gafter(gp[b], "ot")
                        tile = ds(i * (2 * P) + b * P, P)
                        gsig(dve.scalar_tensor_tensor(oT[:, 0:4, tile], bank_u, cols[:, C_GDN:C_GDN + 1],
                                                      sgT[:, :, tile], ALU.mult, ALU.mult))
                    elif stage_name == "att_s":
                        t, w = b, (b + 1) * P
                        gafter(tp, f"s{t}")
                        if t < TT - 1:
                            gafter(ta, f"e{t + 1}")
                        else:
                            gafter(ta, "e0", i - 1)
                        s2 = ps[:, 4:6, :].rearrange("p a n -> p (a n)")
                        sig(td, dve.memset(s2[0:CHUNK, w - CHUNK:w], BIG_NEG))
                        gafter(td, f"mask{t}")
                        sig(td, dve.tensor_reduce(row_stat[:, 3:4], s2[:, 0:w], axis=AX.X, op=ALU.max))
                        gafter(td, f"rowmax{t}")
                        sig(td, dve.tensor_scalar(row_stat[:, 0:1], row_stat[:, 3:4], -1.0, None, ALU.mult))
                    elif stage_name == "att_pv" and b[1] == groups_of[b[0]][-1]:
                        t = b[0]
                        gafter(ta, f"e{t}")
                        sig(td, dve.reciprocal(row_stat[:, 2:3], row_stat[:, 1:2]))
                        gafter(td, f"rinv{t}")
                        gafter(tp, f"pv{t}.{b[1]}")
                        sig(td, dve.tensor_scalar(V[:, t, ds(i, 1), :].rearrange("p a d -> p (a d)"),
                                                  ps[:, 7, 0:V_DIM], row_stat[:, 2:3], None, ALU.mult))

            stages(FIRST_ROUND, 0)
            with dve.Fori(1, TT // 2) as rnd:
                stages(ORDER, rnd)
            stages(AFTER_ROUNDS, TT // 2)

            def x2_gain_low(t):
                dve.wait_ge(x2_turned, t + 1)
                if t >= 2:
                    dve.wait_ge(hf_ready, t - 1)
                pair = 4 + (t % 2) * 2
                view = stage2[t % 2][:, :].rearrange("p (k n) -> p k n", k=KT)
                dve.tensor_tensor(view, ps[:, pair:pair + 2, :].rearrange("p a (k n) -> p (a k) n", n=P),
                                  cols[:, C_FFN:C_FFN + KT].unsqueeze(2).broadcast_to([P, KT, P]),
                                  ALU.mult).then_inc(raw_used, 1)
                dve.wait_ge(hf_high, t + 1)
                dve.tensor_tensor(hf_lo[:, :, tile_cols(t)], view, hf_hi[:, :, tile_cols(t)].bitcast(f32),
                                  ALU.subtract).then_inc(hf_ready, 1)

            for t in range(TT):
                s = (N_X2 + t) % RAW
                dve.wait_ge(op_done, t + 1)
                dve.wait_ge(x_loaded[s], loaded_count(N_X2 + t))
                dve.tensor_tensor(x2[:, t, :], ps[:, (t % 2) * 2:(t % 2) * 2 + 2, :].rearrange("p a n -> p (a n)"),
                                  raw[s][:, :, :].rearrange("p k n -> p (k n)"), ALU.add).then_inc(x2_ready, 1)
                if t >= 1:
                    x2_gain_low(t - 1)
            x2_gain_low(TT - 1)

            def ffn_split_lo(n, count):
                dve.wait_ge(hi_split, count)
                dve.tensor_tensor(w_lo[n % 2][:, :, :], raw[n % RAW][:, :, :], w_hi[n % 2][:, :, :].bitcast(f32),
                                  ALU.subtract).then_inc(raw_used, 1)

            for n in (F0, F0 + 1):
                ffn_split_lo(n, n + 1 - GEMM_LAG)
            for gi, (n0, j0, g) in enumerate(FFN_PLAN):
                with dve.Fori(0, g // 2) as i:
                    for b in range(4):
                        n, s = n0 + b, b // 2
                        dve.wait_ge(gemm_done, i * 4 + (n + 1 - GEMM_LAG))
                        ffn_split_lo(n + 2, i * 4 + (n + 3 - GEMM_LAG))
                        if b % 2 == 1:
                            dve.wait_ge(silu_done, i * 2 + (j0 + s + 1))
                            dve.tensor_tensor(stage2[s][:, :], stage2[s][:, :],
                                              ps[:, 2:4, :].rearrange("p a n -> p (a n)"),
                                              ALU.mult).then_inc(hid_mult, 1)
                            dve.wait_ge(hid_high, i * 2 + (j0 + s + 1))
                            hid = ds(i * 2 + s, 1)
                            dve.tensor_tensor(act_lo[:, hid, :].rearrange("p a n -> p (a n)"), stage2[s][:, :],
                                              act_hi[:, hid, :].rearrange("p a n -> p (a n)").bitcast(f32),
                                              ALU.subtract).then_inc(hid_ready, 1)

                def add_y(m, b, count):
                    dve.wait_ge(y_turned, count)
                    dst = x2[:, :, ds(m * P, P)]
                    pair = (b % 2) * 2
                    dve.tensor_tensor(dst, dst, ps[:, pair:pair + 2, :].rearrange("p a (t n) -> p (a t) n", n=P),
                                      ALU.add).then_inc(x2_added, 1)

                def down_item(b, rnd, split):
                    n = n0 + 2 * g + b
                    dve.wait_ge(gemm_done, rnd * 4 + (n + 1 - GEMM_LAG))
                    if split:
                        ffn_split_lo(n + 2, rnd * 4 + (n + 3 - GEMM_LAG))

                if gi < len(FFN_PLAN) - 1:
                    with dve.Fori(0, KT // 4) as i:
                        for b in range(4):
                            down_item(b, i, True)
                            if b >= 1:
                                add_y(i * 4 + (b - 1), b - 1, i * 4 + (gi * KT + b))
                        add_y(i * 4 + 3, 3, i * 4 + (gi * KT + 4))
                else:
                    for m in range(KT):
                        down_item(m, 0, m + 2 < KT)
                        if m >= 1:
                            add_y(m - 1, m - 1, gi * KT + m)
                    add_y(KT - 1, KT - 1, gi * KT + KT)

        @block.tensor
        def _(pe):
            pe.wait_ge(consts_ready, 1)
            pe.wait_ge(pos_float, 1)
            pe.transpose(ps[:, 7, 0:C_POS], rows, ident[0:C_POS, 0:C_POS])
            pe.transpose(ps[:, 7, C_POS:C_POS + TT], pos_f, ident[0:TT, 0:TT]).then_inc(cols_in_psum, 1)
            for t in range(TT):
                pe.wait_ge(raw_used, t + 1)
                if t >= 2:
                    pe.wait_ge(bank_pair_free, t - 1)
                for k in range(KT):
                    last = pe.transpose(ps[:, (t % 2) * 2 + k // 4, (k % 4) * P:(k % 4 + 1) * P],
                                        x_scaled[t % 2][:, k * P:(k + 1) * P], ident[:, :])
                last.then_inc(x_turned, 1)

            def gemm(whi, wlo, a_hi, a_lo, pair, kts, signal, rows=P):
                for k in range(kts):
                    for w, moving in ((whi, (a_hi, a_lo)), (wlo, (a_hi,))):
                        for a in moving:
                            for h in range(HALVES):
                                last = pe.matmul(ps[0:rows, pair + h, :], w[:, k, 0:rows], a[:, k, h * BANK:(h + 1) * BANK],
                                                 start=(k == 0 and w is whi and a is a_hi),
                                                 stop=(k == kts - 1 and w is wlo))
                last.then_inc(signal, 1)

            pe.wait_ge(h_ready, TT)
            pe.wait_ge(raw_used, N_X + 1)
            gemm(w_hi[0], w_lo[0], act_hi, act_lo, 0, KT, gemm_done, SMALL)
            for m in range(1, M_QKV):
                pe.wait_ge(raw_used, N_X + m + 1)
                pe.wait_ge(bank_pair_free, TT + m - 1)
                gemm(w_hi[m % 2], w_lo[m % 2], act_hi, act_lo, (m % 2) * 2, KT, gemm_done)
                if m == 1:
                    pe.wait_ge(bank_pair_free, TT + 1)
                    for t in range(TT):
                        last = pe.transpose(ps[:, 6, t * SMALL:(t + 1) * SMALL], smallT[:, t * P:(t + 1) * P],
                                            ident[0:SMALL, 0:SMALL])
                    last.then_inc(small_turned, 1)
                if m == M_SMALL + 2:
                    pe.wait_ge(mid_dve.sem, mid_dve.after("g"))
                    for j, tri in enumerate((le, gt, ones)):
                        last = pe.matmul(ps[:, 6, j * 32:(j + 1) * 32], tri[:, :],
                                         g_log[:, :, :].rearrange("p t h -> p (t h)"), start=True, stop=True)
                    last.then_inc(mid_pe.sem, 1)
            with pe.Fori(0, QKV_TILES // 4) as i:
                for b in range(4):
                    m = M_QKV + b
                    pe.wait_ge(raw_used, i * 4 + (N_X + m + 1))
                    pe.wait_ge(bank_pair_free, i * 4 + (TT + m - 1))
                    gemm(w_hi[m % 2], w_lo[m % 2], act_hi, act_lo, (m % 2) * 2, KT, gemm_done)
            pe.wait_ge(bank_pair_free, TT + M_QKV + 1)
            pe.wait_ge(pw_loaded, 4 * 16)
            pe.wait_ge(mid_act.sem, mid_act.after("decays"))
            for p in range(2):
                for h in range(HALVES):
                    last = pe.matmul(ps[:, 4 + 2 * p + h, :], pw[:, p, :], pz[:, p, h * BANK:(h + 1) * BANK],
                                     start=True, stop=True)
                last.then_inc(mid_pe.sem, 1)
            for m in range(M_GATE, IN_ALL):
                pe.wait_ge(raw_used, N_X + m + 1)
                if m < M_GATE + 2:
                    pe.wait_ge(bank_pair_free, TT + m - 1)
                else:
                    pe.wait_ge(gate_pair_free, m - M_GATE - 1)
                gemm(w_hi[m % 2], w_lo[m % 2], act_hi, act_lo, (m % 2) * 2, KT, gemm_done)

            pe.wait_ge(gate_pair_free, GATE_TILES)
            pe.wait_ge(raw_used, N_X + IN_ALL)
            pe.wait_ge(mla_weights, 1)
            pe.wait_ge(mid_act.sem, mid_act.after("pool1"))

            pe.sem_inc(mla_pe.sem, mla_pe.base)
            with pe.Fori(0, TT // 2) as i:
                for b in range(2):
                    bank = 4 * b
                    pe.wait_ge(mla_act.sem, mla_act.after(f"c_sq{b}", i))
                    pe.wait_ge(mla_act.sem, mla_act.after(f"back{b}", i - 1))
                    pe.wait_ge(mla_dve.sem, mla_dve.after(f"kT{b}", i - 1))
                    for k in range(3):
                        pe.matmul(ps[:, bank, k:k + 1], c_sq[b][:, k, :], ones[:, 0:1], start=True, stop=True)
                    for k in range(2):
                        pe.matmul(ps[:, bank + 1, 0:HEADS * QK], cTf[b][:, k, :], wuq[:, k, :],
                                  start=(k == 0), stop=(k == 1))
                    pe.matmul(ps[:, bank + 2, :], cTf[b][:, 2, :], wukv[:, :], start=True,
                              stop=True).then_inc(mla_pe.sem, 1)
                for b in range(2):
                    bank = 4 * b
                    pe.wait_ge(mla_dve.sem, mla_dve.after(f"qk{b}", i))
                    for h in range(HEADS):
                        pe.transpose(ps[0:QK, bank + 3, h * P:(h + 1) * P], qk[b][:, 0, h, :], ident[:, :])
                        last = pe.transpose(ps[0:QK, bank, h * P:(h + 1) * P], qk[b][:, 1, h, :], ident[:, :])
                    last.then_inc(mla_pe.sem, 1)

            for c_ in (gp[0], gp[1], tp):
                pe.sem_inc(c_.sem, len(c_.names))
            pe.wait_ge(mla_act.sem, mla_act.after("back1", TT // 2 - 1))
            pe.wait_ge(mla_dve.sem, mla_dve.after("kT1", TT // 2 - 1))
            pe.wait_ge(mid_act.sem, mid_act.after("decays"))
            def stages(order, rnd):
                def gafter(c, name, rnd=None):
                    pe.wait_ge(c.sem, c.after(name, i if rnd is None else rnd))

                def four(out_bank, lhs, rhs, counter):
                    for h in range(4):
                        last = pe.matmul(ps[:, out_bank, h * P:(h + 1) * P], lhs(h), rhs(h), start=True, stop=True)
                    last.then_inc(counter.sem, 1)

                def four_t(out_bank, src, counter):
                    for h in range(4):
                        last = pe.transpose(ps[:, out_bank, h * P:(h + 1) * P], src(h), ident[:, :])
                    last.then_inc(counter.sem, 1)

                for stage_name, b, back in order:
                    i = rnd - back
                    if stage_name in GDN_STAGES:
                        q = lambda h: qkvf[b][:, h, :]
                        k = lambda h: qkvf[b][:, 4 + h, :]
                        x1 = lambda h: qkvf[b][:, 8 + h, :]
                        on = lambda t3: (lambda h: t3[:, h, :])
                        n_ = lambda p: (lambda h: N_[b][:, p, h, :])
                        cnt = gp[b]
                    if stage_name == "decay":
                        gafter(gd[b], "gtg")
                        four(U[b], on(B_[b]), lambda h: le[:, :], cnt)
                        gafter(ga[b], "sq")
                        for h in range(8):
                            last = pe.matmul(ps[:, W[b], h:h + 1], N_[b][:, h // 4, h % 4, :], ones[:, 0:1],
                                             start=True, stop=True)
                        last.then_inc(cnt.sem, 1)
                    elif stage_name == "kk":
                        gafter(ga[b], "exp")
                        four(U[b], k, k, cnt)
                        gafter(gd[b], "ss")
                        four(W[b], k, q, cnt)
                    elif stage_name == "turn":
                        gafter(gd[b], "att")
                        four_t(W[b], k, cnt)
                        gafter(gd[b], "a0")
                        four_t(U[b], x1, cnt)
                    elif stage_name == "m0":
                        gafter(gd[b], "n0")
                        gafter(gd[b], "kd")
                        four_t(W[b], n_(0), cnt)
                    elif stage_name in X_STAGES:
                        l = int(stage_name[1:])
                        gafter(gg[b], f"b{l}")
                        if l == 1:
                            gafter(ga[b], "m0")
                            gafter(gd[b], "vn")
                        else:
                            gafter(gd[b], f"m{l - 1}")
                        four(U[b], on(B_[b]), on(M_[b]), cnt)
                    elif stage_name in YZ_STAGES:
                        l = int(stage_name[2:])
                        gafter(ga[b], f"x{l}")
                        four(W[b], x1, n_((l - 1) % 2), cnt)
                        if l < LAST:
                            four(U[b], n_((l - 1) % 2), x1, cnt)
                    elif stage_name == "ks":
                        gafter(gd[1 - b], "s", i - 1 if b == 0 else i)
                        gafter(gd[b], f"n{LAST}")
                        four(U[b], k, on(S_), cnt)
                        four(W[b], q, on(S_), cnt)
                    elif stage_name == "tr":
                        gafter(gd[b], "r")
                        four(U[b], n_(0), on(E_[b]), cnt)
                    elif stage_name == "av":
                        gafter(gd[b], "v")
                        four(U[b], on(attn[b]), on(A_[b]), cnt)
                        four(W[b], on(kd[b]), on(A_[b]), cnt)
                    elif stage_name == "ot":
                        gafter(gd[b], "on")
                        four_t(U[b], n_(1), cnt)
                    elif stage_name == "att_s":
                        t, w = b, (b + 1) * P
                        if t == TT - 1:
                            pe.wait_ge(head_loaded, i * 16 + 16)
                            gafter(ta, "e0", i - 1)
                        else:
                            gafter(ta, f"e{t + 1}")
                        for h in range(-(-w // BANK)):
                            n = min(BANK, w - h * BANK)
                            last = pe.matmul(ps[:, 4 + h, 0:n], qh[0:QK, t * P:(t + 1) * P],
                                             kT[0:QK, ds(i, 1), h * BANK:h * BANK + n].rearrange("p a n -> p (a n)"),
                                             start=True, stop=True)
                        last.then_inc(tp.sem, 1)
                    elif stage_name == "att_t":
                        t, g = b
                        if g == 0:
                            gafter(ta, f"e{t}")
                            if t < TT - 1:
                                gafter(ta, f"p{t + 1}.{t + 1 >= 4:d}")
                            else:
                                gafter(ta, "p0.0", i - 1)
                        else:
                            gafter(ta, f"p{t}.0")
                        for j in range(min(4, t + 1 - 4 * g)):
                            kt = 4 * g + j
                            last = pe.transpose(ps[:, 6, j * P:(j + 1) * P], probs[:, kt * P:(kt + 1) * P], ident[:, :])
                        last.then_inc(tp.sem, 1)
                    elif stage_name == "att_pv":
                        t, g = b
                        gafter(ta, f"p{t}.{g}")
                        if g == 0:
                            if t < TT - 1:
                                gafter(td, f"o{t + 1}")
                            else:
                                gafter(td, "o0", i - 1)
                        for j in range(min(4, t + 1 - 4 * g)):
                            kt = 4 * g + j
                            last = pe.matmul(ps[:, 7, 0:V_DIM], probsT[0][:, j, :],
                                             V[:, kt, ds(i, 1), :].rearrange("p a d -> p (a d)"),
                                             start=(kt == 0), stop=(kt == t))
                        last.then_inc(tp.sem, 1)

            stages(FIRST_ROUND, 0)
            with pe.Fori(1, TT // 2) as rnd:
                stages(ORDER, rnd)
            stages(AFTER_ROUNDS, TT // 2)

            pe.wait_ge(td.sem, td.after("o0", TT // 2 - 1))
            pe.wait_ge(ta.sem, ta.after("p0.0", TT // 2 - 1))
            for q4 in range(4):
                for j in range(2):
                    for t2 in range(2):
                        last = pe.transpose(ps[:, 4 + q4, (2 * j + t2) * P:(2 * j + t2 + 1) * P],
                                            V[:, 2 * q4 + t2, 2 * j:2 * j + 2, :].rearrange("p h d -> p (h d)"),
                                            ident[:, :])
                last.then_inc(att_turned, 1)
            for b in range(2):
                pe.wait_ge(gd[b].sem, gd[b].after("out", TT // 2 - 1))
            pe.wait_ge(att_moved, 4)
            pe.wait_ge(w_out_loaded, 16 * KT)

            def turn_x2(t):
                pe.wait_ge(x2_scaled, t + 1)
                if t >= 2:
                    pe.wait_ge(raw_used, N_X2 + t - 1)
                rows_t = raw[(N_X2 + t) % RAW]
                for k in range(KT):
                    last = pe.transpose(ps[:, 4 + (t % 2) * 2 + k // 4, (k % 4) * P:(k % 4 + 1) * P],
                                        rows_t[:, k, :], ident[:, :])
                last.then_inc(x2_turned, 1)

            for t in range(TT):
                if t >= 2:
                    pe.wait_ge(x2_ready, t - 1)
                for k in range(KT):
                    for h in range(HALVES):
                        last = pe.matmul(ps[:, (t % 2) * 2 + h, :], oT[:, k, t * P:(t + 1) * P],
                                         w_out_sb[:, k, h * BANK:(h + 1) * BANK], start=(k == 0), stop=(k == KT - 1))
                last.then_inc(op_done, 1)
                if t >= 1:
                    turn_x2(t - 1)
            turn_x2(TT - 1)

            pe.wait_ge(hf_ready, TT)
            for gi, (n0, j0, g) in enumerate(FFN_PLAN):
                with pe.Fori(0, g // 2) as i:
                    for b in range(4):
                        n, s = n0 + b, b // 2
                        pe.wait_ge(raw_used, i * 4 + (n + 1))
                        if b % 2 == 0:
                            pe.wait_ge(silu_done, i * 2 + (j0 + s))
                        else:
                            pe.wait_ge(hid_mult, i * 2 + (j0 + s))
                        if gi > 0 and b < 2:
                            pe.wait_ge(x2_added, gi * KT)
                        gemm(w_hi[n % 2], w_lo[n % 2], hf_hi, hf_lo, (b % 2) * 2, KT, gemm_done)

                def down_gemm(b, rnd):
                    n = n0 + 2 * g + b
                    pe.wait_ge(raw_used, rnd * 4 + (n + 1))
                    if isinstance(rnd, int) and b == 0:
                        pe.wait_ge(hid_ready, j0 + g)
                    if gi > 0 or b >= 2:
                        pe.wait_ge(y_copied, rnd * 4 + (gi * KT + b - 1))
                    elif not isinstance(rnd, int):
                        pe.wait_ge(y_copied, rnd * 4 + 0)
                    gemm(w_hi[n % 2], w_lo[n % 2], act_hi, act_lo, 4 + (b % 2) * 2, g, gemm_done)

                def turn_y(b, rnd):
                    pe.wait_ge(y_copied, rnd * 4 + (gi * KT + b + 1))
                    if gi > 0 or b >= 2:
                        pe.wait_ge(x2_added, rnd * 4 + (gi * KT + b - 1))
                    elif not isinstance(rnd, int):
                        pe.wait_ge(x2_added, rnd * 4 + 0)
                    for t in range(TT):
                        last = pe.transpose(ps[:, (b % 2) * 2 + t // 4, (t % 4) * P:(t % 4 + 1) * P],
                                            stage2[b % 2][:, t * P:(t + 1) * P], ident[:, :])
                    last.then_inc(y_turned, 1)

                if gi < len(FFN_PLAN) - 1:
                    pe.wait_ge(hid_ready, j0 + g)
                    with pe.Fori(0, KT // 4) as i:
                        for b in range(4):
                            down_gemm(b, i)
                            if b >= 1:
                                turn_y(b - 1, i)
                        turn_y(3, i)
                else:
                    for m in range(KT):
                        down_gemm(m, 0)
                        if m >= 1:
                            turn_y(m - 1, 0)
                    turn_y(KT - 1, 0)



_INS = ["x", "positions", "attn_norm", "w_in", "conv_w", "a_log", "dt_bias", "gdn_out_norm", "pool_w", "pool_scale",
        "q_a_norm", "w_uq", "kv_a_norm", "w_ukv", "q_norm", "k_norm", "w_out", "ffn_norm", "w_gate_up", "w_down"]


def kernel(**inputs):
    import concourse.bacc as bacc
    from concourse.bass_utils import run_bass_kernel_spmd

    nc = bacc.Bacc("TRN2", target_bir_lowering=False, num_devices=1)
    arrays, args = {}, []
    for name in _INS:
        a = np.ascontiguousarray(inputs[name])
        arrays[f"in_{name}"] = a
        args.append(nc.dram_tensor(f"in_{name}", a.shape, mybir.dt.from_np(a.dtype), kind="ExternalInput").ap())
    out = nc.dram_tensor("out_0", (1, SEQ, D_MODEL), mybir.dt.float32, kind="ExternalOutput").ap()
    hybrid_block(nc, *args, out)
    result = run_bass_kernel_spmd(nc, [arrays], core_ids=[0])
    return result.results[0]["out_0"]
```

```python
from contextlib import ExitStack

import numpy as np

import concourse.bass as bass
from concourse import mybir

D_MODEL, SEQ, CHUNK = 1024, 1024, 64
GDN_HEADS, GDN_DIM, CONV_WIDTH = 4, 128, 4
POOL_GROUPS, POOL_DIM, POOL_WINDOWS = 4, 64, (2, 4, 8, 16)
HEADS, NOPE, ROPE, V_DIM, Q_RANK, KV_RANK = 4, 64, 32, 64, 256, 128
EPS, ROPE_THETA = 1e-6, 10000.0

P = 128
QK = NOPE + ROPE
HALF = ROPE // 2
OFF_QKV = 0
OFF_GATE = 3 * GDN_HEADS * GDN_DIM
OFF_A = OFF_GATE + GDN_HEADS * GDN_DIM
OFF_POOL = OFF_A + 2 * GDN_HEADS
OFF_CQ = OFF_POOL + POOL_GROUPS * POOL_DIM
OFF_CKV = OFF_CQ + Q_RANK
OFF_KR = OFF_CKV + KV_RANK
FFN_HIDDEN = ((8 * D_MODEL // 3 + 255) // 256) * 256

KT = D_MODEL // P
TT = SEQ // P
BANK = 512
HALVES = SEQ // BANK
QKV_TILES = 3 * GDN_HEADS
GATE_TILES = GDN_HEADS
FIRST_TILES = [OFF_CQ, OFF_CQ + P, OFF_CKV, OFF_POOL, OFF_POOL + P]
IN_TILES = len(FIRST_TILES) + QKV_TILES + GATE_TILES
HID_TILES = FFN_HIDDEN // P
GROUPS = [8, 8, 6]
SMALL = 2 * GDN_HEADS + ROPE
RAW, SPLIT = 4, 2
LEVELS = [1 << s for s in range(7)]
BIG_NEG = -1.0e30
assert sum(GROUPS) == HID_TILES and TT == 8 and HEADS == 4 and GDN_HEADS == 4


class Steps:

    def __init__(self, sem, names, ahead=False):
        self.sem, self.names = sem, list(names)
        self.base = len(self.names) if ahead else 0
        assert len(set(self.names)) == len(self.names)

    def after(self, name, rnd=0):
        return self.base + rnd * len(self.names) + (self.names.index(name) + 1)


def hybrid_block(nc, x, positions, attn_norm, w_in, conv_w, a_log, dt_bias, gdn_out_norm, pool_w, pool_scale,
                 q_a_norm, w_uq, kv_a_norm, w_ukv, q_norm, k_norm, w_out, ffn_norm, w_gate_up, w_down, out):
    f32, f32r, i32 = mybir.dt.float32, mybir.dt.float32r, mybir.dt.int32
    ALU, ACT, AX = mybir.AluOpType, mybir.ActivationFunctionType, mybir.AxisListType
    ds = bass.ds

    class Region:

        def __init__(self, start):
            self.at = start

        def take(self, name, shape, dt=f32):
            t = nc.alloc_sbuf_tensor_at(name, shape, dt, offset=self.at)
            self.at += -(-int(np.prod(shape[1:])) * 4 // 32) * 32
            return t

    SBUF_START, SBUF_END = 16512, 224 * 1024
    c = Region(SBUF_START)
    ident = c.take("ident", [P, P])
    le = c.take("le", [P, P])
    gt = c.take("gt", [P, P])
    ones = c.take("ones", [P, P])
    cols = c.take("cols", [P, 80])
    ab_rows = c.take("ab_rows", [P, 2, GDN_HEADS])
    small_tok = c.take("small_tok", [P, TT, SMALL])
    kr_ss = c.take("kr_ss", [P, TT])
    trig = c.take("trig", [P, 2, TT, HALF])
    g_log = c.take("g_log", [P, TT, GDN_HEADS])
    beta = c.take("beta", [P, TT, GDN_HEADS])
    decays = c.take("decays", [P, 3, TT, GDN_HEADS])
    half_neg = c.take("half_neg", [P, 16])
    half_pos = c.take("half_pos", [P, 16])
    recip_cnt = c.take("recip_cnt", [P, 16])
    ssq = c.take("ssq", [P, TT])
    meansq = c.take("meansq", [P, TT])
    rstd = c.take("rstd", [P, TT])
    tok_sc = [c.take(f"tok_sc{b}", [P, 64]) for b in range(2)]
    row_stats = [c.take(f"row_stat{j}", [P, 4]) for j in range(2)]
    R1 = c.at
    R2 = R1 + 64 * 1024
    R3 = R2 + 64 * 1024

    r = Region(R1)
    act_hi = r.take("act_hi", [P, KT, SEQ], f32r)
    act_lo = r.take("act_lo", [P, KT, SEQ], f32r)
    r = Region(R1)
    oT = r.take("oT", [P, KT, SEQ])
    qT = r.take("qT", [P, HEADS, SEQ])
    kT = r.take("kT", [P, HEADS, SEQ])
    w_out_sb = Region(R1 + 32 * 1024).take("w_out_sb", [P, KT, D_MODEL])
    r = Region(R2)
    qkvT = r.take("qkvT", [P, QKV_TILES, SEQ])
    sgT = r.take("sgT", [P, GATE_TILES, SEQ])
    r = Region(R2)
    hf_hi = r.take("hf_hi", [P, KT, SEQ], f32r)
    hf_lo = r.take("hf_lo", [P, KT, SEQ], f32r)
    r = Region(R3)
    w_hi = [r.take(f"w_hi{s}", [P, KT, P], f32r) for s in range(SPLIT)]
    w_lo = [r.take(f"w_lo{s}", [P, KT, P], f32r) for s in range(SPLIT)]
    raw = [r.take(f"raw{s}", [P, KT, P]) for s in range(RAW)]
    R3_REST = r.at
    cT = r.take("cT", [P, 3, SEQ])
    wuq = r.take("wuq", [P, 2, HEADS * QK])
    wukv = r.take("wukv", [P, HEADS * (NOPE + V_DIM)])
    pw = r.take("pw", [P, 2, P])
    pz = r.take("pz", [P, 2, SEQ])
    stage = [r.take(f"stage{s}", [P, SEQ]) for s in range(2)]
    assert r.at <= SBUF_END, r.at - SBUF_END
    r = Region(R3_REST)
    x2 = r.take("x2", [P, TT, D_MODEL])
    stage2 = [r.take(f"stage2_{s}", [P, SEQ]) for s in range(2)]
    assert r.at <= SBUF_END, r.at - SBUF_END
    x2_sq = Region(R3).take("x2_sq", [P, D_MODEL])
    V = Region(R3_REST + 26 * 1024).take("V", [P, TT, HEADS, V_DIM])
    r = Region(R3_REST + 34 * 1024)
    masks = r.take("masks", [P, len(LEVELS), P])
    qk_gain = Region(r.at).take("qk_gain", [P, 2, QK])
    qh = r.take("qh", [P, SEQ])
    assert r.at <= SBUF_END, r.at - SBUF_END
    r = Region(R3)
    cTf = [r.take(f"cTf{b}", [P, 3, P]) for b in range(4)]
    qk_sq = [r.take(f"qk_sq{b}", [P, HEADS, QK + NOPE]) for b in range(4)]
    qk = [r.take(f"qk{b}", [P, 2, HEADS, QK]) for b in range(4)]
    rot = [r.take(f"rot{b}", [P, 4, 2 * HEADS, HALF]) for b in range(2)]
    assert r.at <= R3_REST
    r = Region(R3_REST + 18 * 1024)
    mla_sc = [r.take(f"mla_sc{b}", [P, 40]) for b in range(4)]
    r = Region(R3)
    qkvf = [r.take(f"qkvf{b}", [P, 12, P]) for b in range(2)]
    E_ = [r.take(f"E{b}", [P, 4, P]) for b in range(2)]
    attn = [r.take(f"attn{b}", [P, 4, P]) for b in range(2)]
    A_ = [r.take(f"A{b}", [P, 4, P]) for b in range(2)]
    B_ = [r.take(f"B{b}", [P, 4, P]) for b in range(2)]
    N_ = [r.take(f"N{b}", [P, 2, 4, P]) for b in range(2)]
    M_ = [r.take(f"M{b}", [P, 4, P]) for b in range(2)]
    kd = [r.take(f"kd{b}", [P, 4, P]) for b in range(2)]
    Vn = [r.take(f"Vn{b}", [P, 4, P]) for b in range(2)]
    S_ = r.take("S", [P, 4, P])
    probs = r.take("probs", [P, SEQ])
    assert r.at <= R3_REST + 26 * 1024, r.at - R3_REST
    probsT = [r.take(f"probsT{g}", [P, 4, P]) for g in range(1)]
    assert r.at <= R3_REST + 26 * 1024 + 0, r.at - R3_REST - 26 * 1024
    rows = qkvT[0:70, 3, 0:P]
    pos_i = nc.alloc_sbuf_tensor_at("pos_i", [P, P], i32, offset=R2 + 4 * SEQ * 4)
    pos_f = qkvT[0:TT, 5, 0:P]
    inv_freq = qkvT[:, 6, 0:HALF]
    ang = qkvT[:, 7, 0:P]
    turns = qkvT[:, 8, 0:P]
    turns_i = nc.alloc_sbuf_tensor_at("turns_i", [P, P], i32, offset=R2 + 9 * SEQ * 4)
    wrap = qkvT[:, 10, 0:2 * P]
    sin_in = qkvT[:, 11, 0:2 * P]
    smallT = qkvT[0:SMALL, 3, :]
    c_sq = qkvT[:, 5:8, :]
    lat_ms, lat_inv, lat_rstd = (tok_sc[0][:, 16 * j:16 * j + 16] for j in range(3))
    small_raw = sgT[:, 3, 0:KT * SMALL].rearrange("p (k n) -> p k n", k=KT)
    mid = sgT[:, 3, 320:576].rearrange("p (a t h) -> p a t h", a=8, t=TT)
    kr_sq = sgT[:, 3, 576:832].rearrange("p (t n) -> p t n", t=TT)
    assert KT * SMALL <= 320
    x_sq = qkvT[:, 0, :]
    x_scaled = [qkvT[:, 1 + s, :] for s in range(2)]
    C_CONV, C_ATTN, C_FFN, C_QA, C_KVA, C_GDN, C_POOL, C_POS, C_QK = 0, 48, 56, 64, 66, 67, 68, 70, 78

    ctx = ExitStack()
    with ctx:
        def sem(name):
            return ctx.enter_context(nc.semaphore(name))

        ps = ctx.enter_context(nc.psum_tensor("ps", [P, 8, BANK], f32))

        rows_loaded = sem("rows_loaded")
        x_loaded = [sem(f"raw_loaded{s}") for s in range(RAW)]
        prep_loaded = sem("mla_weights_loaded")
        small_loaded = sem("small_loaded")
        small_turned = sem("small_turned")
        consts_ready = sem("consts_ready")
        pool_chain, dve_chain, act_chain = sem("pool_chain"), sem("dve_chain"), sem("act_chain")
        cols_in_psum = sem("cols_in_psum")
        cols_ready = sem("cols_ready")
        pos_float = sem("pos_float")
        sin_args = sem("sin_args")
        trig_ready = sem("trig_ready")
        x_sumsq = sem("x_sumsq")
        x_rstd = sem("x_rstd")
        raw_used = sem("raw_used")
        x_turned = sem("x_turned")
        bank_pair_free = sem("bank_pair_free")
        gate_pair_free = sem("gate_pair_free")
        stage_read = sem("stage_read")
        h_ready = sem("h_ready")
        hi_split = sem("hi_split")
        gemm_done = sem("gemm_done")

        w_out_loaded = [sem(f"w_out_loaded{j}") for j in range(2)]
        att_turned = sem("att_turned")
        att_moved = sem("att_moved")
        op_done = sem("out_proj_done")
        x2_ready = sem("x2_ready")
        x2_sumsq, x2_rstd = sem("x2_sumsq"), sem("x2_rstd")
        x2_scaled = sem("x2_scaled")
        x2_turned = sem("x2_turned")
        hf_high, hf_ready = sem("hf_high"), sem("hf_ready")
        silu_done = sem("silu_done")
        hid_mult = sem("hid_mult")
        hid_high, hid_ready = sem("hid_high"), sem("hid_ready")
        y_copied = sem("y_copied")
        y_turned = sem("y_turned")
        x2_added = sem("x2_added")
        stored = sem("stored")
        mla_weights = sem("mla_weights")
        pw_loaded = sem("pw_loaded")
        chunk_loaded = [sem(f"chunk_loaded{b}") for b in range(2)]
        head_loaded = sem("head_loaded")

        mid_pe = Steps(sem("mid_pe"), ["decays", "pool0", "pool1"])
        mid_act = Steps(sem("mid_act"), ["exp_abs", "exp_alog", "exp_b", "ln", "kr_sq", "decays", "pool0", "pool1"])
        mid_dve = Steps(sem("mid_dve"), ["abs", "one_plus", "g"])
        mla_pe = Steps(sem("mla_pe"), [f"front{b}" for b in range(4)] + [f"back{b}" for b in range(4)], ahead=True)
        mla_act = Steps(sem("mla_act"), [f"{n}{b}" for n in ("cTf", "sq", "turned") for b in range(4)], ahead=True)
        MLA_STEPS = [("a", 0), ("a", 1), ("b", 0), ("a", 2), ("b", 1), ("a", 3), ("b", 2), ("b", 3)]
        mla_dve = Steps(sem("mla_dve"), [{"a": f"qk_ms{b}", "b": f"qk{b}"}[n] for n, b in MLA_STEPS], ahead=True)
        mla_pool = Steps(sem("mla_pool"), [f"qk_pow{b}" for b in range(4)])
        LINKS_MLA = 4 * 6
        lat_squared = sem("latents_squared")
        lat_summed = sem("latents_summed")
        lat_mean = sem("latents_mean")
        lat_ready = sem("latents_rstd")
        LAST = len(LEVELS) - 1
        X_STAGES = [f"x{l}" for l in range(1, LAST + 1)]
        YZ_STAGES = [f"yz{l}" for l in range(1, LAST + 1)]
        levels = [st for pair in zip(X_STAGES, YZ_STAGES) for st in pair]
        GDN_STAGES = ["pre", "decay", "stats", "kk", "turn", "m0"] + levels + ["ks", "tr", "av", "oms", "on", "ot"]
        yz_pe = [n for l in range(1, LAST + 1) for n in ([f"x{l}", f"y{l}"] + ([f"z{l}"] if l < LAST else []))]
        nm_dve = [n for l in range(1, LAST + 1) for n in ([f"n{l}"] + ([f"m{l}"] if l < LAST else []))]
        gp = [Steps(sem(f"gdn_pe{b}"), ["decay", "norms", "kk", "qk", "kT", "vT", "m0"] + yz_pe
                    + ["ks", "qs", "tr", "av", "ds", "ot"], ahead=True) for b in range(2)]
        ga = [Steps(sem(f"gdn_act{b}"), ["sq", "exp", "m0"] + X_STAGES + ["osq"], ahead=True) for b in range(2)]
        gd = [Steps(sem(f"gdn_dve{b}"), ["gtg", "et", "ss", "rc", "c", "att", "a0", "a", "kd", "vn", "rqs", "r2", "n0"]
                    + nm_dve + ["r0", "r", "o1", "v", "s", "o", "osum", "oms0", "oms", "of", "on", "out"], ahead=True)
              for b in range(2)]
        gg = [Steps(sem(f"gdn_pool{b}"), ["mask", "rq", "nk"] + [f"b{l}" for l in range(LAST + 1)] + ["sd", "pow"],
                    ahead=True) for b in range(2)]
        q_tiles = list(range(TT - 1, -1, -1))
        groups_of = {t: (range(2) if t >= 4 else range(1)) for t in q_tiles}
        head_part = [("att_s", TT - 1, 0)]
        for t in q_tiles:
            for g in groups_of[t]:
                head_part.append(("att_t", (t, g), 0))
                if t > 0 and g == groups_of[t][-1]:
                    head_part.append(("att_s", t - 1, 0))
                head_part.append(("att_pv", (t, g), 0))
        tp = Steps(sem("att_pe"), [f"s{w}" if st == "att_s" else f"{st[4:]}{w[0]}.{w[1]}" for st, w, _ in head_part],
                   ahead=True)
        ta = Steps(sem("att_act"), [n for t in q_tiles for n in [f"e{t}"] + [f"p{t}.{g}" for g in groups_of[t]]],
                   ahead=True)
        td = Steps(sem("att_dve"), [f"{n}{w if st == 'att_s' else w[0]}" for st, w, _ in head_part
                                    if st == "att_s" or st == "att_pv" and w[1] == groups_of[w[0]][-1]
                                    for n in (("mask", "rowmax", "max") if st == "att_s" else ("rinv", "o"))],
                   ahead=True)
        SHIFT = 8
        late = len(GDN_STAGES) - SHIFT
        slot1 = [(st, 1, 1) for st in GDN_STAGES[late:]] + [(st, 1, 0) for st in GDN_STAGES[:late]]
        chunk_part = [e for st, e1 in zip(GDN_STAGES, slot1) for e in ((st, 0, 0), e1)]
        ORDER = []
        for n, e in enumerate(chunk_part):
            ORDER += [e] + head_part[n * len(head_part) // len(chunk_part):(n + 1) * len(head_part) // len(chunk_part)]
        FIRST_ROUND = [e for e in ORDER if not e[2]]
        AFTER_ROUNDS = [e for e in ORDER if e[2]]
        OP_EARLY = [(t, k) for half in range(2) for t in range(2) for k in range(half * 4, half * 4 + 4)]
        op_pair = [0, 6] + [2 * (1 - t % 2) for t in range(2, TT)]
        U, W = [0, 2], [1, 3]

        def heads_of(m):
            return m[:, :].unsqueeze(1).broadcast_to([P, 4, P])

        def per_head(v):
            return v.unsqueeze(2).broadcast_to([P, 4, P])

        def flat(t):
            return t[:, :, :].rearrange("p h n -> p (h n)")

        def heads_view(bank):
            return bank.rearrange("p (h n) -> p h n", h=4)

        class Chain:

            def __init__(self, eng, sm):
                self.eng, self.sem, self.n, self.extra = eng, sm, 0, 0

            def __call__(self, op):
                op.then_inc(self.sem, 1)
                self.n += 1
                self.eng.wait_ge(self.sem, self.n + self.extra)

            def start_round(self, rnd, per_round):
                self.first, self.per, self.extra = self.n, per_round, rnd * per_round

            def end_rounds(self, count):
                assert self.n - self.first == self.per, (self.n - self.first, self.per)
                self.n = self.first + self.per * count
                self.extra = 0

        def tile_cols(t):
            return ds(t * P, P)

        def proj_col(m):
            return FIRST_TILES[m - 1] if m <= len(FIRST_TILES) else OFF_QKV + (m - 1 - len(FIRST_TILES)) * P

        M_CQ, M_CKV, M_POOL, M_QKV = 1, 3, 4, 1 + len(FIRST_TILES)
        M_GATE = M_QKV + QKV_TILES
        M_SMALL = 2
        IN_ALL = M_GATE + GATE_TILES
        N_X = TT
        N_X2 = N_X + IN_ALL
        F0 = N_X2 + TT
        GEMM_LAG = N_X + TT
        FFN_PLAN = []
        for g in GROUPS:
            n0 = FFN_PLAN[-1][0] + 2 * FFN_PLAN[-1][2] + KT if FFN_PLAN else F0
            FFN_PLAN.append((n0, sum(gr for _, _, gr in FFN_PLAN), g))

        def loaded_count(n):
            return 16 * (n // RAW + 1) - (16 if n % RAW == 0 else 0)

        w_in_v = w_in[0].rearrange("(k p) n -> p k n", p=P)

        block = ctx.enter_context(nc.Block())

        @block.sync
        def _(sp):
            def load_x(t):
                if t >= RAW:
                    sp.wait_ge(raw_used, t - RAW + 1)
                sp.dma_start(raw[t % RAW][:, :, :].rearrange("p k n -> p (k n)"),
                             x[0, t * P:(t + 1) * P, :]).then_inc(x_loaded[t % RAW], 16)

            for t in range(RAW):
                load_x(t)
            sp.dma_start(small_raw[:, :, 0:2 * GDN_HEADS], w_in_v[:, :, OFF_A:OFF_POOL]).then_inc(small_loaded, 16)
            sp.dma_start(small_raw[:, :, 2 * GDN_HEADS:SMALL],
                         w_in_v[:, :, OFF_KR:OFF_KR + ROPE]).then_inc(small_loaded, 16)
            sp.dma_start(ab_rows[:, 0, :], a_log[0].partition_broadcast(P)).then_inc(prep_loaded, 16)
            sp.dma_start(ab_rows[:, 1, :], dt_bias[0].partition_broadcast(P)).then_inc(prep_loaded, 16)
            sp.dma_start(wuq[:, :, :], w_uq[0].rearrange("(k p) n -> p k n", p=P)).then_inc(prep_loaded, 16)
            sp.dma_start(wukv[:, :], w_ukv[0]).then_inc(prep_loaded, 16)
            sp.dma_start(qk_gain[:, 0, :], q_norm[0].partition_broadcast(P)).then_inc(prep_loaded, 16)
            sp.dma_start(qk_gain[:, 1, :], k_norm[0].partition_broadcast(P)).then_inc(prep_loaded, 16)
            for t in range(RAW, TT):
                load_x(t)

            sp.wait_ge(consts_ready, 1)
            for g in range(POOL_GROUPS):
                lo = (g % 2) * POOL_DIM
                sp.dma_start(pw[lo:lo + POOL_DIM, g // 2, lo:lo + POOL_DIM], pool_w[0, g]).then_inc(pw_loaded, 16)
            for j, gain in enumerate((q_norm, k_norm)):
                sp.dma_start(cols[0:NOPE, C_QK + j:C_QK + j + 1],
                             gain[0, 0:NOPE].rearrange("(p o) -> p o", o=1)).then_inc(pw_loaded, 16)

            def load_in_tile(m, s):
                sp.wait_ge(raw_used, N_X + m - RAW + 1)
                sp.dma_start(raw[s][:, :, :], w_in_v[:, :, ds(proj_col(m), P)]).then_inc(x_loaded[s], 16)

            for m in range(1, M_QKV):
                load_in_tile(m, (N_X + m) % RAW)
            with sp.Fori(0, QKV_TILES // 4) as i:
                for b in range(4):
                    load_in_tile(M_QKV + b + i * 4, (N_X + M_QKV + b) % RAW)
            for m in range(M_GATE, IN_ALL):
                load_in_tile(m, (N_X + m) % RAW)

            sp.wait_ge(mla_act.sem, mla_act.after("turned3", TT // 4 - 1))
            def load_chunk(b, i):
                sp.wait_ge(gp[b].sem, gp[b].after("qs", i - 1))
                sp.dma_start(qkvf[b][:, :, :], qkvT[:, :, ds(i * (2 * P) + b * P, P)]).then_inc(chunk_loaded[b], 16)

            def load_head(i):
                sp.wait_ge(tp.sem, tp.after("s0", i - 1))
                sp.dma_start(qh[0:QK, :], qT[0:QK, ds(i, 1), :].rearrange("p a n -> p (a n)")).then_inc(head_loaded, 16)

            load_head(0)
            load_chunk(0, 0)
            load_chunk(1, 0)
            with sp.Fori(1, TT // 2) as i:
                load_chunk(0, i)
                load_head(i)
                load_chunk(1, i)

            for half in range(2):
                if half == 0:
                    sp.wait_ge(head_loaded, 16 * HEADS)
                else:
                    sp.wait_ge(tp.sem, tp.after("s0", TT // 2 - 1))
                for k in range(half * 4, half * 4 + 4):
                    sp.dma_start(w_out_sb[:, k, :], w_out[0, k * P:(k + 1) * P, :]).then_inc(w_out_loaded[half], 16)
            for b in range(2):
                sp.wait_ge(gd[b].sem, gd[b].after("out", TT // 2 - 1))
            sp.wait_ge(td.sem, td.after("o0", TT // 2 - 1))
            for t in range(TT):
                n = N_X2 + t
                if t >= RAW:
                    sp.wait_ge(raw_used, n - RAW + 1)
                sp.dma_start(raw[n % RAW][:, :, :].rearrange("p k n -> p (k n)"),
                             x[0, t * P:(t + 1) * P, :]).then_inc(x_loaded[n % RAW], 16)
            w_gu_v = w_gate_up[0].rearrange("(k p) n -> p k n", p=P)
            w_dn_v = w_down[0].rearrange("(j p) n -> p j n", p=P)
            for gi, (n0, j0, g) in enumerate(FFN_PLAN):
                with sp.Fori(0, g // 2) as i:
                    for b in range(4):
                        sp.wait_ge(raw_used, i * 4 + (n0 + b - RAW + 1))
                        col = (b % 2) * FFN_HIDDEN + (j0 + b // 2) * P
                        sp.dma_start(raw[(n0 + b) % RAW][:, :, :],
                                     w_gu_v[:, :, ds(i * (2 * P) + col, P)]).then_inc(x_loaded[(n0 + b) % RAW], 16)
                n1 = n0 + 2 * g

                def load_down(m, b, count):
                    sp.wait_ge(raw_used, count - RAW + 1)
                    sp.dma_start(raw[(n1 + b) % RAW][:, 0:g, :],
                                 w_dn_v[:, j0:j0 + g, ds(m * P, P)]).then_inc(x_loaded[(n1 + b) % RAW], 16)

                if gi < len(FFN_PLAN) - 1:
                    with sp.Fori(0, KT // 4) as i:
                        for b in range(4):
                            load_down(i * 4 + b, b, i * 4 + (n1 + b))
                else:
                    def store(m):
                        sp.wait_ge(x2_added, gi * KT + m + 1)
                        sp.dma_start(out[0].rearrange("(t p) n -> p t n", p=P)[:, :, m * P:(m + 1) * P],
                                     x2[:, :, m * P:(m + 1) * P]).then_inc(stored, 16)

                    for m in range(KT):
                        load_down(m, m, n1 + m)
                        if m >= RAW:
                            store(m - RAW)
                    for m in range(KT - RAW, KT):
                        store(m)
            sp.wait_ge(stored, 16 * KT)

        @block.gpsimd
        def _(pool):
            link = Chain(pool, pool_chain)
            pool.memset(ones[:, :], 1.0)
            pool.memset(half_neg[:, :], -0.5)
            pool.memset(half_pos[:, :], 0.5)
            pool.memset(pw[:, :, :], 0.0)
            pool.memset(cols[:, C_QK:C_QK + 2], 1.0)
            link(pool.memset(ident[:, :], 0.0))
            link(pool.memset(le[:, :], 1.0))
            link(pool.memset(gt[:, :], 1.0))
            pool.affine_select(out=ident[:, :], in_=ident[:, :], compare_op=ALU.not_equal, fill=1.0,
                               base=0, pattern=[[-1, P]], channel_multiplier=1)
            pool.affine_select(out=le[:, :], in_=le[:, :], compare_op=ALU.is_ge, fill=0.0,
                               base=0, pattern=[[1, P]], channel_multiplier=-1)
            pool.affine_select(out=gt[:, :], in_=gt[:, :], compare_op=ALU.is_gt, fill=0.0,
                               base=0, pattern=[[-1, P]], channel_multiplier=1)
            for j in range(16):
                pool.memset(recip_cnt[:, j:j + 1], 1.0 / (j + 1))
            for j in range(HALF):
                last = pool.memset(inv_freq[:, j:j + 1],
                                   float(np.float32(ROPE_THETA) ** np.float32(-2.0 * j / ROPE)))
            last.then_inc(consts_ready, 1)
            for t in range(TT):
                pool.wait_ge(x_sumsq, t + 1)
                link(pool.tensor_scalar(meansq[:, t:t + 1], ssq[:, t:t + 1], 1.0 / D_MODEL, EPS, ALU.mult, ALU.add))
                pool.tensor_tensor(rstd[:, t:t + 1], meansq[:, t:t + 1], half_neg[:, 0:1],
                                   ALU.pow).then_inc(x_rstd, 1)

            for l, s in enumerate(LEVELS):
                blocks = masks[:, l, :].rearrange("p (b u) -> p b u", u=2 * s)
                link(pool.memset(masks[:, l, :], 0.0))
                link(pool.memset(blocks[:, :, s:2 * s], 1.0))
                nb = P // (2 * s)
                link(pool.affine_select(out=blocks, in_=blocks, compare_op=ALU.is_ge, fill=0.0, base=0,
                                        pattern=[[-2 * s, nb], [0, 2 * s]], channel_multiplier=1))
                link(pool.affine_select(out=blocks, in_=blocks, compare_op=ALU.is_ge, fill=0.0, base=s - 1,
                                        pattern=[[2 * s, nb], [0, 2 * s]], channel_multiplier=-1))

            pool.wait_ge(lat_mean, 1)
            pool.tensor_tensor(lat_rstd, lat_ms, half_neg[:, :], ALU.pow).then_inc(lat_ready, 1)
            with pool.Fori(0, TT // 4) as i:
                for b in range(4):
                    pool.wait_ge(mla_dve.sem, mla_dve.after(f"qk_ms{b}", i))
                    pool.tensor_tensor(mla_sc[b][:, 24:32], mla_sc[b][:, 16:24], half_neg[:, 0:8],
                                       ALU.pow).then_inc(mla_pool.sem, 1)

            for c_ in gg:
                pool.sem_inc(c_.sem, c_.base)
            def stages(order, rnd):
                for stage_name, b, back in order:
                    i = rnd - back
                    if stage_name == "decay":
                        pool.wait_ge(ga[b].sem, ga[b].after("exp", i))
                        pool.tensor_tensor(E_[b][:, :, :], E_[b][:, :, :], heads_of(le), ALU.mult).then_inc(gg[b].sem, 1)
                    elif stage_name == "stats":
                        sc = tok_sc[b]
                        pool.wait_ge(gd[b].sem, gd[b].after("ss", i))
                        pool.tensor_tensor(sc[:, 12:16], sc[:, 0:4], half_neg[:, 0:4], ALU.pow).then_inc(gg[b].sem, 1)
                        pool.tensor_tensor(sc[:, 8:12], sc[:, 4:8], half_pos[:, 0:4], ALU.pow).then_inc(gg[b].sem, 1)
                    elif stage_name == "kk":
                        pool.wait_ge(gd[b].sem, gd[b].after("a", i))
                        pool.tensor_tensor(B_[b][:, :, :], A_[b][:, :, :], heads_of(masks[:, 0, :]),
                                           ALU.mult).then_inc(gg[b].sem, 1)
                    elif stage_name == "m0" or stage_name in X_STAGES[:-1]:
                        if stage_name == "m0":
                            l = 1
                            pool.wait_ge(gd[b].sem, gd[b].after("n0", i))
                        else:
                            l = int(stage_name[1:]) + 1
                            pool.wait_ge(gp[b].sem, gp[b].after(stage_name, i))
                        pool.tensor_tensor(B_[b][:, :, :], A_[b][:, :, :], heads_of(masks[:, l, :]),
                                           ALU.mult).then_inc(gg[b].sem, 1)
                    elif stage_name == "ks":
                        pool.wait_ge(gd[b].sem, gd[b].after("et", i))
                        pool.wait_ge(gp[b].sem, gp[b].after("qs", i))
                        pool.tensor_tensor(S_[:, :, :], S_[:, :, :], per_head(tok_sc[b][:, 20:24]),
                                           ALU.mult).then_inc(gg[b].sem, 1)
                    elif stage_name == "oms":
                        sc = tok_sc[b]
                        pool.wait_ge(gd[b].sem, gd[b].after("oms", i))
                        pool.tensor_tensor(sc[:, 32:36], sc[:, 28:32], half_neg[:, 0:4], ALU.pow).then_inc(gg[b].sem, 1)

            stages(FIRST_ROUND, 0)
            with pool.Fori(1, TT // 2) as rnd:
                stages(ORDER, rnd)
            stages(AFTER_ROUNDS, TT // 2)

            for t in range(TT):
                pool.wait_ge(x2_sumsq, t + 1)
                link(pool.tensor_scalar(meansq[:, t:t + 1], ssq[:, t:t + 1], 1.0 / D_MODEL, EPS, ALU.mult, ALU.add))
                pool.tensor_tensor(rstd[:, t:t + 1], meansq[:, t:t + 1], half_neg[:, 0:1],
                                   ALU.pow).then_inc(x2_rstd, 1)

        @block.scalar
        def _(act):
            link = Chain(act, act_chain)
            act.dma_start(rows[0:48, :], conv_w[0].rearrange("j (f p) -> (j f) p", p=P)).then_inc(rows_loaded, 16)
            act.dma_start(rows[48:56, :], attn_norm[0].rearrange("(f p) -> f p", p=P)).then_inc(rows_loaded, 16)
            act.dma_start(rows[56:64, :], ffn_norm[0].rearrange("(f p) -> f p", p=P)).then_inc(rows_loaded, 16)
            act.dma_start(rows[64:66, :], q_a_norm[0].rearrange("(f p) -> f p", p=P)).then_inc(rows_loaded, 16)
            act.dma_start(rows[66:67, :], kv_a_norm[0].rearrange("(f p) -> f p", p=P)).then_inc(rows_loaded, 16)
            act.dma_start(rows[67:68, :], gdn_out_norm[0].rearrange("(f p) -> f p", p=P)).then_inc(rows_loaded, 16)
            act.dma_start(rows[68:70, :], pool_scale[0].rearrange("(f p) -> f p", p=P)).then_inc(rows_loaded, 16)
            act.dma_start(pos_i[0:TT, :], positions[0].rearrange("(f p) -> f p", p=P)).then_inc(rows_loaded, 16)

            def x_square(t):
                act.wait_ge(x_loaded[t % RAW], 16 * (t // RAW + 1))
                if t >= 1:
                    act.wait_ge(x_sumsq, t)
                act.activation(x_sq, raw[t % RAW][:, :, :].rearrange("p k n -> p (k n)"), ACT.Square,
                               accum_out=ssq[:, t:t + 1]).then_inc(x_sumsq, 1)

            AHEAD = 3
            for t in range(AHEAD):
                x_square(t)
            for t in range(TT):
                if t + AHEAD < TT:
                    x_square(t + AHEAD)
                if t == TT - 2:
                    act.wait_ge(small_loaded, 2 * 16)
                    act.activation(w_hi[0][:, :, 0:SMALL], small_raw, ACT.Copy).then_inc(hi_split, 1)
                act.wait_ge(bank_pair_free, t + 1)
                act.activation(act_hi[:, :, tile_cols(t)], stage[t % 2][:, :].rearrange("p (k n) -> p k n", k=KT),
                               ACT.Copy).then_inc(stage_read, 1)
            def split_hi(m, slot, rawslot, rnd):
                act.wait_ge(x_loaded[rawslot], rnd)
                act.activation(w_hi[slot][:, :, :], raw[rawslot][:, :, :], ACT.Copy).then_inc(hi_split, 1)

            def in_round(m):
                return loaded_count(N_X + m)

            split_hi(1, 1, 1, in_round(1))
            act.wait_ge(sin_args, 1)
            act.activation(trig[:, :, :, :].rearrange("p a t f -> p (a t f)"), sin_in, ACT.Sin).then_inc(trig_ready, 1)

            for m in range(M_QKV):
                act.wait_ge(gemm_done, m + 1)
                split_hi(m + 2, m % 2, (N_X + m + 2) % RAW, in_round(m + 2))
                if M_CQ <= m < M_POOL:
                    act.wait_ge(bank_pair_free, TT + m + 1)
                    act.activation(c_sq[:, m - 1, :], cT[:, m - 1, :], ACT.Square).then_inc(lat_squared, 1)
                if m == M_SMALL:
                    act.wait_ge(mid_dve.sem, mid_dve.after("abs"))
                    act.activation(mid[:, 2, :, :], mid[:, 1, :, :], ACT.Exp, scale=-1.0).then_inc(mid_act.sem, 1)
                    act.activation(mid[:, 5, 0, :], ab_rows[:, 0, :], ACT.Exp).then_inc(mid_act.sem, 1)
                    act.activation(mid[:, 6, :, :], small_tok[:, :, GDN_HEADS:2 * GDN_HEADS], ACT.Exp,
                                   scale=-1.0).then_inc(mid_act.sem, 1)
                    act.wait_ge(mid_dve.sem, mid_dve.after("one_plus"))
                    act.activation(mid[:, 3, :, :], mid[:, 3, :, :], ACT.Ln).then_inc(mid_act.sem, 1)
                    act.activation(kr_sq, small_tok[:, :, 2 * GDN_HEADS:SMALL], ACT.Square).then_inc(mid_act.sem, 1)
                if m == M_SMALL + 2:
                    act.wait_ge(mid_pe.sem, mid_pe.after("decays"))
                    act.activation(decays[:, :, :, :].rearrange("p a t h -> p (a t h)"),
                                   ps[:, 6, 0:3 * TT * GDN_HEADS], ACT.Exp).then_inc(mid_act.sem, 1)

            def silu_qkv(f, s):
                act.wait_ge(bank_pair_free, f + (TT + M_QKV + 1))
                act.activation(qkvT[:, ds(f, 1), :].rearrange("p a n -> p (a n)"), stage[s][:, :],
                               ACT.Silu).then_inc(stage_read, 1)

            with act.Fori(0, QKV_TILES // 4) as i:
                for b in range(4):
                    m = M_QKV + b
                    act.wait_ge(gemm_done, i * 4 + (m + 1))
                    split_hi(None, m % 2, (N_X + m + 2) % RAW, in_round(m + 2) + i * 16)
                    silu_qkv(b + i * 4, m % 2)
            for m in range(M_GATE, IN_ALL):
                act.wait_ge(gemm_done, m + 1)
                if m + 2 < IN_ALL:
                    split_hi(m + 2, m % 2, (N_X + m + 2) % RAW, in_round(m + 2))
                pair = (m % 2) * 2
                act.activation(sgT[:, m - M_GATE, :], ps[:, pair:pair + 2, :].rearrange("p a n -> p (a n)"),
                               ACT.Silu).then_inc(gate_pair_free, 1)

            for p in range(2):
                act.wait_ge(mid_pe.sem, mid_pe.after(f"pool{p}"))
                act.activation(oT[:, 4 + p, :], ps[:, 4 + 2 * p:6 + 2 * p, :].rearrange("p a n -> p (a n)"), ACT.Copy,
                               scale=cols[:, C_POOL + p:C_POOL + p + 1]).then_inc(mid_act.sem, 1)

            act.sem_inc(mla_act.sem, mla_act.base)
            act.wait_ge(lat_ready, 1)
            with act.Fori(0, TT // 4) as i:
                for b in range(4):
                    tile = ds(i * (4 * P) + b * P, P)
                    act.wait_ge(mla_pe.sem, mla_pe.after(f"front{b}", i - 1))
                    act.activation(cTf[b][:, :, :], cT[:, :, tile], ACT.Copy).then_inc(mla_act.sem, 1)
                for b in range(4):
                    kv = ps[:, 2 * b + 1, :].rearrange("p (h d) -> p h d", h=HEADS)
                    act.wait_ge(mla_dve.sem, mla_dve.after(f"qk_ms{b}", i - 1))
                    act.wait_ge(mla_pe.sem, mla_pe.after(f"front{b}", i))
                    act.activation(qk_sq[b][:, :, 0:QK], ps[:, 2 * b, 0:HEADS * QK].rearrange(
                        "p (h d) -> p h d", h=HEADS), ACT.Square)
                    act.activation(qk_sq[b][:, :, QK:QK + NOPE], kv[:, :, 0:NOPE], ACT.Square)
                    act.activation(V[:, ds(i * 4 + b, 1), :, :].rearrange("p a h d -> p (a h) d"), kv[:, :, NOPE:],
                                   ACT.Copy, scale=lat_rstd[:, ds(i * 8 + (2 * b + 1), 1)]).then_inc(mla_act.sem, 1)
                for b in range(4):
                    tile = ds(i * (4 * P) + b * P, P)
                    act.wait_ge(mla_pe.sem, mla_pe.after(f"back{b}", i))
                    for j, dst in enumerate((qT, kT)):
                        op = act.activation(dst[0:QK, :, tile], ps[0:QK, 2 * b + j, :].rearrange(
                            "p (h d) -> p h d", h=HEADS), ACT.Copy, scale=cols[0:QK, C_QK + j:C_QK + j + 1])
                    op.then_inc(mla_act.sem, 1)

            act.sem_inc(ga[0].sem, len(ga[0].names))
            act.sem_inc(ga[1].sem, len(ga[1].names))
            act.sem_inc(ta.sem, len(ta.names))
            act.wait_ge(mla_dve.sem, mla_dve.after("qk3", TT // 4 - 1))
            def stages(order, rnd):
                def gsig(b, ins):
                    ins.then_inc(ga[b].sem, 1)

                def gafter(c, name, rnd=None):
                    act.wait_ge(c.sem, c.after(name, i if rnd is None else rnd))

                for stage_name, b, back in order:
                    i = rnd - back
                    if stage_name == "pre":
                        act.wait_ge(chunk_loaded[b], i * 16 + 16)
                        gafter(gp[b], "ot", i - 1)
                        gsig(b, act.activation(N_[b][:, :, :, :].rearrange("p a h n -> p (a h) n"),
                                               qkvf[b][:, 0:8, :], ACT.Square))
                    elif stage_name == "decay":
                        gafter(gp[b], "decay")
                        gsig(b, act.activation(flat(E_[b]), ps[:, U[b], :], ACT.Exp))
                    elif stage_name == "m0":
                        gafter(gp[b], "m0")
                        gsig(b, act.activation(flat(M_[b]), ps[:, W[b], :], ACT.Copy))
                    elif stage_name in X_STAGES:
                        gafter(gp[b], stage_name)
                        gsig(b, act.activation(qkvf[b][:, 8:12, :].rearrange("p h n -> p (h n)"), ps[:, U[b], :],
                                               ACT.Copy))
                    elif stage_name == "av":
                        gafter(gd[b], "o")
                        gsig(b, act.activation(flat(Vn[b]), flat(M_[b]), ACT.Square))
                    elif stage_name == "att_s":
                        t, w = b, (b + 1) * P
                        gafter(td, f"max{b}")
                        if b < TT - 1:
                            gafter(tp, f"t{b + 1}.{b + 1 >= 4:d}")
                        else:
                            gafter(tp, "t0.0", i - 1)
                        act.activation(probs[:, 0:w], ps[:, 4:6, :].rearrange("p a n -> p (a n)")[:, 0:w], ACT.Exp,
                                       bias=row_stats[t % 2][:, 0:1], accum_out=row_stats[t % 2][:, 1:2]).then_inc(ta.sem, 1)
                    elif stage_name == "att_t":
                        t, g = b
                        n = min(4, t + 1 - 4 * g) * P
                        gafter(tp, f"t{t}.{g}")
                        act.activation(flat(probsT[0])[:, 0:n], ps[:, 6, 0:n], ACT.Copy).then_inc(ta.sem, 1)

            stages(FIRST_ROUND, 0)
            with act.Fori(1, TT // 2) as rnd:
                stages(ORDER, rnd)
            for q4 in range(4):
                act.wait_ge(att_turned, q4 + 1)
                act.activation(oT[:, 6:8, q4 * 2 * P:(q4 + 1) * 2 * P],
                               ps[:, 4 + q4, :].rearrange("p (j n) -> p j n", j=2), ACT.Copy).then_inc(att_moved, 1)
            stages(AFTER_ROUNDS, TT // 2)

            def x2_high(t):
                act.wait_ge(raw_used, N_X2 + t + 1)
                act.activation(hf_hi[:, :, tile_cols(t)], stage2[t % 2][:, :].rearrange("p (k n) -> p k n", k=KT),
                               ACT.Copy).then_inc(hf_high, 1)

            for t in range(TT):
                s = (N_X2 + t) % RAW
                act.wait_ge(x2_ready, t + 1)
                if t >= 1:
                    act.wait_ge(x2_sumsq, t)
                act.activation(x2_sq[:, :], x2[:, t, :], ACT.Square, accum_out=ssq[:, t:t + 1]).then_inc(x2_sumsq, 1)
                act.wait_ge(x2_rstd, t + 1)
                act.activation(raw[s][:, :, :].rearrange("p k n -> p (k n)"), x2[:, t, :], ACT.Copy,
                               scale=rstd[:, t:t + 1]).then_inc(x2_scaled, 1)
                if t >= 1:
                    x2_high(t - 1)
            x2_high(TT - 1)

            def ffn_split_hi(n, count):
                act.wait_ge(x_loaded[n % RAW], count)
                act.activation(w_hi[n % 2][:, :, :], raw[n % RAW][:, :, :], ACT.Copy).then_inc(hi_split, 1)

            for n in (F0, F0 + 1):
                ffn_split_hi(n, loaded_count(n))
            for gi, (n0, j0, g) in enumerate(FFN_PLAN):
                with act.Fori(0, g // 2) as i:
                    for b in range(4):
                        n, s = n0 + b, b // 2
                        act.wait_ge(gemm_done, i * 4 + (n + 1 - GEMM_LAG))
                        ffn_split_hi(n + 2, loaded_count(n + 2) + i * 16)
                        if b % 2 == 0:
                            act.wait_ge(hid_ready, i * 2 + (j0 + s))
                            act.activation(stage2[s][:, :], ps[:, 0:2, :].rearrange("p a n -> p (a n)"),
                                           ACT.Silu).then_inc(silu_done, 1)
                        else:
                            act.wait_ge(hid_mult, i * 2 + (j0 + s + 1))
                            act.activation(act_hi[:, ds(i * 2 + s, 1), :].rearrange("p a n -> p (a n)"),
                                           stage2[s][:, :], ACT.Copy).then_inc(hid_high, 1)

                def down_item(b, rnd, split):
                    n = n0 + 2 * g + b
                    act.wait_ge(gemm_done, rnd * 4 + (n + 1 - GEMM_LAG))
                    if split:
                        ffn_split_hi(n + 2, loaded_count(n + 2) + rnd * 16)
                    if gi > 0 or b >= 2:
                        act.wait_ge(y_turned, rnd * 4 + (gi * KT + b - 1))
                    elif not isinstance(rnd, int):
                        act.wait_ge(y_turned, rnd * 4 + 0)
                    act.activation(stage2[b % 2][:, :], ps[:, 4 + (b % 2) * 2:6 + (b % 2) * 2, :].rearrange(
                        "p a n -> p (a n)"), ACT.Copy).then_inc(y_copied, 1)

                if gi < len(FFN_PLAN) - 1:
                    with act.Fori(0, KT // 4) as i:
                        for b in range(4):
                            down_item(b, i, True)
                else:
                    for m in range(KT):
                        down_item(m, 0, m + 2 < KT)

        @block.vector
        def _(dve):
            link = Chain(dve, dve_chain)

            dve.wait_ge(rows_loaded, 8 * 16)
            dve.tensor_copy(pos_f, pos_i[0:TT, :]).then_inc(pos_float, 1)
            dve.wait_ge(cols_in_psum, 1)
            link(dve.tensor_copy(cols[:, 0:C_POS + TT], ps[:, 7, 0:C_POS + TT]))

            def x_scale(t):
                dve.wait_ge(x_rstd, t + 1)
                if t >= 2:
                    dve.wait_ge(x_turned, t - 1)
                dve.tensor_scalar(x_scaled[t % 2], raw[t % RAW][:, :, :].rearrange("p k n -> p (k n)"),
                                  rstd[:, t:t + 1], None, ALU.mult).then_inc(raw_used, 1)

            def x_gain(t):
                dve.wait_ge(x_turned, t + 1)
                if t >= 2:
                    dve.wait_ge(h_ready, t - 1)
                pair = (t % 2) * 2
                dve.tensor_tensor(stage[t % 2][:, :].rearrange("p (k n) -> p k n", k=KT),
                                  ps[:, pair:pair + 2, :].rearrange("p a (k n) -> p (a k) n", n=P),
                                  cols[:, C_ATTN:C_ATTN + KT].unsqueeze(2).broadcast_to([P, KT, P]),
                                  ALU.mult).then_inc(bank_pair_free, 1)

            def x_low(t):
                dve.wait_ge(stage_read, t + 1)
                dve.tensor_tensor(act_lo[:, :, tile_cols(t)], stage[t % 2][:, :].rearrange("p (k n) -> p k n", k=KT),
                                  act_hi[:, :, tile_cols(t)].bitcast(f32), ALU.subtract).then_inc(h_ready, 1)

            x_scale(0)
            for t in range(TT):
                if t + 1 < TT:
                    x_scale(t + 1)
                if t >= 1:
                    x_low(t - 1)
                if t == TT - 1:
                    dve.wait_ge(hi_split, 1)
                    dve.tensor_tensor(w_lo[0][:, :, 0:SMALL], small_raw, w_hi[0][:, :, 0:SMALL].bitcast(f32),
                                      ALU.subtract).then_inc(raw_used, 1)
                x_gain(t)
            x_low(TT - 1)

            def split_lo(m, slot, rawslot):
                dve.wait_ge(hi_split, m + 1)
                dve.tensor_tensor(w_lo[slot][:, :, :], raw[rawslot][:, :, :], w_hi[slot][:, :, :].bitcast(f32),
                                  ALU.subtract).then_inc(raw_used, 1)

            def sig(c, ins):
                ins.then_inc(c.sem, 1)

            def mid_after(c, name):
                dve.wait_ge(c.sem, c.after(name))

            def decays_and_betas():
                dve.wait_ge(prep_loaded, 6 * 16)
                dve.wait_ge(small_turned, 1)
                link(dve.tensor_copy(small_tok[:, :, :].rearrange("p t n -> p (t n)"), ps[:, 6, 0:TT * SMALL]))
                link(dve.tensor_tensor(mid[:, 0, :, :], small_tok[:, :, 0:GDN_HEADS],
                                       ab_rows[:, 1, :].unsqueeze(1).broadcast_to([P, TT, GDN_HEADS]), ALU.add))
                sig(mid_dve, dve.scalar_tensor_tensor(mid[:, 1, :, :], mid[:, 0, :, :], -1.0, mid[:, 0, :, :],
                                                      ALU.mult, ALU.max))
                for k in range(2):
                    dve.tensor_scalar(wuq[:, k, :], wuq[:, k, :], cols[:, C_QA + k:C_QA + k + 1], None, ALU.mult)
                dve.tensor_scalar(wukv[:, :], wukv[:, :], cols[:, C_KVA:C_KVA + 1], None,
                                  ALU.mult).then_inc(mla_weights, 1)
                mid_after(mid_act, "exp_abs")
                sig(mid_dve, dve.tensor_scalar(mid[:, 3, :, :], mid[:, 2, :, :], 1.0, None, ALU.add))
                mid_after(mid_act, "exp_b")
                link(dve.tensor_scalar(mid[:, 7, :, :], mid[:, 6, :, :], 1.0, None, ALU.add))
                link(dve.reciprocal(beta[:, :, :], mid[:, 7, :, :]))
                mid_after(mid_act, "ln")
                link(dve.scalar_tensor_tensor(mid[:, 4, :, :], mid[:, 0, :, :], 0.0, mid[:, 3, :, :], ALU.max, ALU.add))
                sig(mid_dve, dve.scalar_tensor_tensor(g_log[:, :, :], mid[:, 4, :, :], -1.0,
                                                      mid[:, 5, 0, :].unsqueeze(1).broadcast_to([P, TT, GDN_HEADS]),
                                                      ALU.mult, ALU.mult))
                mid_after(mid_act, "kr_sq")
                link(dve.tensor_reduce(kr_ss[:, :], kr_sq, axis=AX.X, op=ALU.add))

            def pair_of(m):
                return ps[:, (m % 2) * 2:(m % 2) * 2 + 2, :].rearrange("p a n -> p (a n)")

            split_lo(1, 1, 1)
            ang_v = ang.rearrange("p (t f) -> p t f", t=TT)
            link(dve.tensor_tensor(ang_v, cols[:, C_POS:C_POS + TT].unsqueeze(2).broadcast_to([P, TT, HALF]),
                                   inv_freq.unsqueeze(1).broadcast_to([P, TT, HALF]), ALU.mult))
            two_pi = 2.0 * np.pi
            c1 = 6.28125
            c2 = float(np.float32(np.floor((two_pi - c1) * 2.0 ** 20) / 2.0 ** 20))
            c3 = two_pi - c1 - c2
            link(dve.tensor_scalar(turns, ang, 1.0 / two_pi, None, ALU.mult))
            link(dve.tensor_copy(turns_i[:, :], turns))
            link(dve.tensor_copy(turns, turns_i[:, :]))
            for part in (c1, c2, c3):
                link(dve.scalar_tensor_tensor(ang, turns, -part, ang, ALU.mult, ALU.add))
            link(dve.tensor_copy(sin_in[:, P:2 * P], ang))
            link(dve.tensor_scalar(sin_in[:, 0:P], ang, np.pi / 2, None, ALU.add))
            for bound, op, shift in ((np.pi, ALU.is_gt, -two_pi), (-np.pi, ALU.is_lt, two_pi)):
                link(dve.tensor_scalar(wrap, sin_in, bound, shift, op, ALU.mult))
                link(dve.tensor_tensor(sin_in, sin_in, wrap, ALU.add))
            dve.tensor_scalar(sin_in, sin_in, 3.1415925, -3.1415925, ALU.min, ALU.max).then_inc(sin_args, 1)

            for m in range(M_QKV):
                dve.wait_ge(gemm_done, m + 1)
                split_lo(m + 2, m % 2, (N_X + m + 2) % RAW)
                if m == 0:
                    dve.tensor_copy(smallT, ps[0:SMALL, 0:2, :].rearrange("p a n -> p (a n)")).then_inc(
                        bank_pair_free, 1)
                elif m < M_POOL:
                    dve.tensor_copy(cT[:, m - 1, :], pair_of(m)).then_inc(bank_pair_free, 1)
                    if m == M_SMALL:
                        decays_and_betas()
                else:
                    p = m - M_POOL
                    px, sums = sgT[:, 0, :], [sgT[:, 1, :], sgT[:, 2, :]]
                    dve.tensor_copy(px, pair_of(m)).then_inc(bank_pair_free, 1)
                    dve.wait_ge(bank_pair_free, TT + m + 1)
                    src, width, n = px, 1, 0
                    lows = {}
                    while width < POOL_WINDOWS[2 * p + 1]:
                        r0 = 64 if 2 * width > POOL_WINDOWS[2 * p] else 0
                        dst = sums[n % 2]
                        dve.tensor_copy(dst[r0:P, 0:width], src[r0:P, 0:width])
                        link(dve.tensor_tensor(dst[r0:P, width:SEQ], src[r0:P, width:SEQ], src[r0:P, 0:SEQ - width],
                                               ALU.add))
                        width *= 2
                        lows[width] = dst
                        src, n = dst, n + 1
                    for g in range(2):
                        w = POOL_WINDOWS[2 * p + g]
                        rr = slice(64 * g, 64 * g + 64)
                        s_w = lows[w]
                        dve.scalar_tensor_tensor(pz[rr, p, w - 1:SEQ], s_w[rr, w - 1:SEQ], 1.0 / w, px[rr, w - 1:SEQ],
                                                 ALU.mult, ALU.subtract)
                        link(dve.tensor_tensor(pz[rr, p, 0:w - 1], s_w[rr, 0:w - 1], recip_cnt[rr, 0:w - 1], ALU.mult))
                        link(dve.tensor_tensor(pz[rr, p, 0:w - 1], pz[rr, p, 0:w - 1], px[rr, 0:w - 1], ALU.subtract))

            dve.wait_ge(lat_summed, 1)
            for j, width in enumerate((Q_RANK, KV_RANK)):
                op = dve.tensor_scalar(lat_ms.rearrange("p (t j) -> p t j", j=2)[:, :, j:j + 1],
                                       ps[:, 5, 0:2 * TT].rearrange("p (t j) -> p t j", j=2)[:, :, j:j + 1],
                                       1.0 / width, EPS, ALU.mult, ALU.add)
            op.then_inc(lat_mean, 1)
            dve.wait_ge(lat_mean, 1)
            link(dve.reciprocal(lat_inv, lat_ms))

            with dve.Fori(0, QKV_TILES // 4) as i:
                link.start_round(i, 3 * 4)
                for b in range(4):
                    m, s = M_QKV + b, (M_QKV + b) % 2
                    dve.wait_ge(gemm_done, i * 4 + (m + 1))
                    split_lo(m + 2 + i * 4, s, (N_X + m + 2) % RAW)
                    dve.wait_ge(stage_read, i * 4 + (TT + b - 1))
                    src, dst = pair_of(m), stage[s]

                    def tap(j):
                        return cols[:, ds(C_CONV + j * QKV_TILES + b + i * 4, 1)]

                    link(dve.tensor_scalar(dst[:, :], src, tap(3), None, ALU.mult))
                    for d in (1, 2, 3):
                        op = dve.scalar_tensor_tensor(dst[:, d:SEQ], src[:, 0:SEQ - d], tap(3 - d), dst[:, d:SEQ],
                                                      ALU.mult, ALU.add)
                        if d < 3:
                            link(op)
                    op.then_inc(bank_pair_free, 1)
            link.end_rounds(QKV_TILES // 4)
            for m in range(M_GATE, IN_ALL - 2):
                split_lo(m + 2, m % 2, (N_X + m + 2) % RAW)

            dve.wait_ge(gemm_done, IN_ALL)
            dve.wait_ge(stage_read, TT + QKV_TILES)
            dve.sem_inc(mla_dve.sem, mla_dve.base)
            dve.wait_ge(lat_ready, 1)
            with dve.Fori(0, TT // 4) as i:
                link.start_round(i, LINKS_MLA)

                def mafter(c, name, rnd=None):
                    dve.wait_ge(c.sem, c.after(name, i if rnd is None else rnd))

                for part, b in MLA_STEPS:
                    t, sc = i * 4 + b, mla_sc[b]
                    of_q, of_kv = ds(i * 8 + 2 * b, 1), ds(i * 8 + (2 * b + 1), 1)
                    if part == "a":
                        mafter(mla_act, f"sq{b}")
                        dve.tensor_reduce(sc[:, 0:4], qk_sq[b][:, :, 0:QK], axis=AX.X, op=ALU.add)
                        link(dve.tensor_reduce(sc[:, 4:8], qk_sq[b][:, :, QK:QK + NOPE], axis=AX.X, op=ALU.add))
                        dve.tensor_scalar(sc[:, 8:12], sc[:, 0:4], lat_inv[:, of_q], None, ALU.mult)
                        link(dve.tensor_scalar(sc[:, 12:16], sc[:, 4:8], lat_inv[:, of_kv], kr_ss[:, ds(t, 1)],
                                               ALU.mult, ALU.add))
                        sig(mla_dve, dve.tensor_scalar(sc[:, 16:24], sc[:, 8:16], 1.0 / QK, EPS, ALU.mult, ALU.add))
                    else:
                        mafter(mla_pool, f"qk_pow{b}")
                        dve.tensor_scalar(sc[:, 32:36], sc[:, 24:28], lat_rstd[:, of_q], float(QK) ** -0.5,
                                          ALU.mult, ALU.mult)
                        link(dve.tensor_scalar(sc[:, 36:40], sc[:, 28:32], lat_rstd[:, of_kv], None, ALU.mult))
                        mafter(mla_pe, f"back{b}", i - 1)
                        q_, k_ = qk[b][:, 0, :, :], qk[b][:, 1, :, :]
                        dve.tensor_tensor(q_, ps[:, 2 * b, 0:HEADS * QK].rearrange("p (h d) -> p h d", h=HEADS),
                                          sc[:, 32:36].unsqueeze(2).broadcast_to([P, HEADS, QK]), ALU.mult)
                        dve.tensor_tensor(k_[:, :, 0:NOPE],
                                          ps[:, 2 * b + 1, :].rearrange("p (h d) -> p h d", h=HEADS)[:, :, 0:NOPE],
                                          sc[:, 36:40].unsqueeze(2).broadcast_to([P, HEADS, NOPE]), ALU.mult)
                        link(dve.tensor_tensor(k_[:, :, NOPE:QK],
                                               small_tok[:, ds(t, 1), 2 * GDN_HEADS:SMALL].broadcast_to(
                                                   [P, HEADS, ROPE]),
                                               sc[:, 28:32].unsqueeze(2).broadcast_to([P, HEADS, ROPE]), ALU.mult))
                        link(dve.tensor_tensor(qk[b][:, :, :, NOPE:QK], qk[b][:, :, :, NOPE:QK],
                                               qk_gain[:, :, NOPE:QK].unsqueeze(2).broadcast_to([P, 2, HEADS, ROPE]),
                                               ALU.mult))
                        both = qk[b][:, :, :, :].rearrange("p a h d -> p (a h) d")
                        x1, x2_ = both[:, :, NOPE:NOPE + HALF], both[:, :, NOPE + HALF:QK]
                        cos = trig[:, 0, ds(t, 1), :].broadcast_to([P, 2 * HEADS, HALF])
                        sin = trig[:, 1, ds(t, 1), :].broadcast_to([P, 2 * HEADS, HALF])
                        ro = rot[b % 2]
                        dve.tensor_tensor(ro[:, 0, :, :], x1, cos, ALU.mult)
                        dve.tensor_tensor(ro[:, 1, :, :], x2_, sin, ALU.mult)
                        dve.tensor_tensor(ro[:, 2, :, :], x2_, cos, ALU.mult)
                        link(dve.tensor_tensor(ro[:, 3, :, :], x1, sin, ALU.mult))
                        dve.tensor_tensor(x1, ro[:, 0, :, :], ro[:, 1, :, :], ALU.subtract)
                        sig(mla_dve, dve.tensor_tensor(x2_, ro[:, 2, :, :], ro[:, 3, :, :], ALU.add))
            link.end_rounds(TT // 4)

            for c_ in (gd[0], gd[1], td):
                dve.sem_inc(c_.sem, len(c_.names))
            dve.wait_ge(mla_act.sem, mla_act.after("turned3", TT // 4 - 1))
            link(dve.memset(S_[:, :, :], 0.0))
            def stages(order, rnd):
                def gafter(c, name, rnd=None):
                    dve.wait_ge(c.sem, c.after(name, i if rnd is None else rnd))

                def decay(which, b):
                    return decays[:, which, ds(i * 2 + b, 1), :].rearrange("p a h -> p (a h)")

                for stage_name, b, back in order:
                    i = rnd - back
                    if stage_name in GDN_STAGES:
                        sc, bank_u, bank_w = tok_sc[b], heads_view(ps[:, U[b], :]), heads_view(ps[:, W[b], :])
                        e, a, bm, m_, n_ = E_[b], A_[b], B_[b], M_[b], N_[b]

                        def own(name, rnd=None):
                            gafter(gd[b], name, rnd)

                        def gsig(ins):
                            sig(gd[b], ins)
                    if stage_name == "pre":
                        own("out", i - 1)
                        gsig(dve.tensor_tensor(bm[:, :, :], heads_of(gt),
                                               per_head(g_log[:, ds(i * 2 + b, 1), :].rearrange("p a h -> p (a h)")),
                                               ALU.mult))
                        gafter(gg[b], "sd", i - 1)
                        gsig(dve.tensor_copy(sc[:, 20:24], decay(2, b)))
                    elif stage_name == "stats":
                        gafter(gp[b], "norms")
                        gsig(dve.tensor_scalar(sc[:, 0:8], ps[:, W[b], 0:8], EPS, None, ALU.add))
                        own("ss")
                        gsig(dve.reciprocal(sc[:, 24:28], sc[:, 4:8]))
                        own("rc")
                        gsig(dve.tensor_tensor(sc[:, 16:20], sc[:, 24:28],
                                               beta[:, ds(i * 2 + b, 1), :].rearrange("p a h -> p (a h)"), ALU.mult))
                    elif stage_name == "kk":
                        gafter(gg[b], "mask")
                        gafter(gp[b], "qk")
                        own("c")
                        gsig(dve.tensor_tensor(attn[b][:, :, :], bank_w, e[:, :, :], ALU.mult))
                        gsig(dve.tensor_tensor(a[:, :, :], bank_u, e[:, :, :], ALU.mult))
                        own("a0")
                        gsig(dve.tensor_tensor(a[:, :, :], a[:, :, :], per_head(sc[:, 16:20]), ALU.mult))
                    elif stage_name == "turn":
                        gafter(gp[b], "vT")
                        gsig(dve.tensor_tensor(kd[b][:, :, :], bank_w, per_head(decay(1, b)), ALU.mult))
                        gafter(gg[b], "nk")
                        gsig(dve.tensor_tensor(Vn[b][:, :, :], bank_u, per_head(sc[:, 8:12]), ALU.mult))
                        gsig(dve.tensor_scalar(sc[:, 12:16], sc[:, 12:16], float(GDN_DIM) ** -0.5, None, ALU.mult))
                        own("rqs")
                        gsig(dve.tensor_tensor(sc[:, 36:40], sc[:, 12:16], sc[:, 12:16], ALU.mult))
                    elif stage_name == "m0":
                        gafter(gg[b], "b0")
                        gafter(gp[b], "norms")
                        gsig(dve.tensor_tensor(n_[:, 0, :, :], heads_of(ident), bm[:, :, :], ALU.subtract))
                    elif stage_name in YZ_STAGES:
                        l = int(stage_name[2:])
                        gafter(gp[b], f"y{l}")
                        gsig(dve.tensor_tensor(n_[:, l % 2, :, :], n_[:, (l - 1) % 2, :, :], bank_w, ALU.subtract))
                        if l < LAST:
                            gafter(gp[b], f"z{l}")
                            gsig(dve.tensor_tensor(m_[:, :, :], m_[:, :, :], bank_u, ALU.subtract))
                    elif stage_name == "ks":
                        gafter(gp[b], "ks")
                        gsig(dve.tensor_tensor(e[:, :, :], bank_u, per_head(decay(0, b)), ALU.mult))
                        own("r0")
                        gsig(dve.tensor_tensor(e[:, :, :], Vn[b][:, :, :], e[:, :, :], ALU.subtract))
                        gafter(gp[b], "qs")
                        gsig(dve.tensor_tensor(bm[:, :, :], bank_w, per_head(decay(0, b)), ALU.mult))
                    elif stage_name == "tr":
                        gafter(gp[b], "tr")
                        gsig(dve.tensor_tensor(a[:, :, :], bank_u, per_head(sc[:, 16:20]), ALU.mult))
                    elif stage_name == "av":
                        gafter(gp[b], "ds")
                        gafter(gg[b], "sd")
                        gsig(dve.tensor_tensor(S_[:, :, :], S_[:, :, :], bank_w, ALU.add))
                        own("o1")
                        gsig(dve.tensor_tensor(m_[:, :, :], bm[:, :, :], bank_u, ALU.add))
                    elif stage_name == "oms":
                        gafter(ga[b], "osq")
                        gsig(dve.tensor_reduce(sc[:, 24:28], Vn[b][:, :, :], axis=AX.X, op=ALU.add))
                        own("osum")
                        gsig(dve.scalar_tensor_tensor(sc[:, 28:32], sc[:, 24:28], 1.0 / GDN_DIM, sc[:, 36:40],
                                                      ALU.mult, ALU.mult))
                        own("oms0")
                        gsig(dve.tensor_scalar(sc[:, 28:32], sc[:, 28:32], EPS, None, ALU.add))
                    elif stage_name == "on":
                        gafter(gg[b], "pow")
                        gsig(dve.tensor_tensor(sc[:, 40:44], sc[:, 32:36], sc[:, 12:16], ALU.mult))
                        own("of")
                        gsig(dve.tensor_tensor(n_[:, 1, :, :], m_[:, :, :], per_head(sc[:, 40:44]), ALU.mult))
                    elif stage_name == "ot":
                        gafter(gp[b], "ot")
                        tile = ds(i * (2 * P) + b * P, P)
                        gsig(dve.scalar_tensor_tensor(oT[:, 0:4, tile], bank_u, cols[:, C_GDN:C_GDN + 1],
                                                      sgT[:, :, tile], ALU.mult, ALU.mult))
                    elif stage_name == "att_s":
                        t, w = b, (b + 1) * P
                        gafter(tp, f"s{t}")
                        if t < TT - 1:
                            gafter(ta, f"e{t + 1}")
                        else:
                            gafter(ta, "e0", i - 1)
                        s2 = ps[:, 4:6, :].rearrange("p a n -> p (a n)")
                        sig(td, dve.memset(s2[0:CHUNK, w - CHUNK:w], BIG_NEG))
                        gafter(td, f"mask{t}")
                        sig(td, dve.tensor_reduce(row_stats[t % 2][:, 3:4], s2[:, 0:w], axis=AX.X, op=ALU.max))
                        gafter(td, f"rowmax{t}")
                        sig(td, dve.tensor_scalar(row_stats[t % 2][:, 0:1], row_stats[t % 2][:, 3:4], -1.0, None, ALU.mult))
                    elif stage_name == "att_pv" and b[1] == groups_of[b[0]][-1]:
                        t = b[0]
                        gafter(ta, f"e{t}")
                        sig(td, dve.reciprocal(row_stats[t % 2][:, 2:3], row_stats[t % 2][:, 1:2]))
                        gafter(td, f"rinv{t}")
                        gafter(tp, f"pv{t}.{b[1]}")
                        sig(td, dve.tensor_scalar(V[:, t, ds(i, 1), :].rearrange("p a d -> p (a d)"),
                                                  ps[:, 7, 0:V_DIM], row_stats[t % 2][:, 2:3], None, ALU.mult))

            stages(FIRST_ROUND, 0)
            with dve.Fori(1, TT // 2) as rnd:
                stages(ORDER, rnd)
            stages(AFTER_ROUNDS, TT // 2)

            def x2_gain_low(t):
                dve.wait_ge(x2_turned, t + 1)
                if t >= 2:
                    dve.wait_ge(hf_ready, t - 1)
                pair = 4 + (t % 2) * 2
                view = stage2[t % 2][:, :].rearrange("p (k n) -> p k n", k=KT)
                dve.tensor_tensor(view, ps[:, pair:pair + 2, :].rearrange("p a (k n) -> p (a k) n", n=P),
                                  cols[:, C_FFN:C_FFN + KT].unsqueeze(2).broadcast_to([P, KT, P]),
                                  ALU.mult).then_inc(raw_used, 1)
                dve.wait_ge(hf_high, t + 1)
                dve.tensor_tensor(hf_lo[:, :, tile_cols(t)], view, hf_hi[:, :, tile_cols(t)].bitcast(f32),
                                  ALU.subtract).then_inc(hf_ready, 1)

            for t in range(TT):
                s = (N_X2 + t) % RAW
                dve.wait_ge(op_done, t + 1)
                dve.wait_ge(x_loaded[s], loaded_count(N_X2 + t))
                dve.tensor_tensor(x2[:, t, :], ps[:, op_pair[t]:op_pair[t] + 2, :].rearrange("p a n -> p (a n)"),
                                  raw[s][:, :, :].rearrange("p k n -> p (k n)"), ALU.add).then_inc(x2_ready, 1)
                if t >= 1:
                    x2_gain_low(t - 1)
            x2_gain_low(TT - 1)

            def ffn_split_lo(n, count):
                dve.wait_ge(hi_split, count)
                dve.tensor_tensor(w_lo[n % 2][:, :, :], raw[n % RAW][:, :, :], w_hi[n % 2][:, :, :].bitcast(f32),
                                  ALU.subtract).then_inc(raw_used, 1)

            for n in (F0, F0 + 1):
                ffn_split_lo(n, n + 1 - GEMM_LAG)
            for gi, (n0, j0, g) in enumerate(FFN_PLAN):
                with dve.Fori(0, g // 2) as i:
                    for b in range(4):
                        n, s = n0 + b, b // 2
                        dve.wait_ge(gemm_done, i * 4 + (n + 1 - GEMM_LAG))
                        ffn_split_lo(n + 2, i * 4 + (n + 3 - GEMM_LAG))
                        if b % 2 == 1:
                            dve.wait_ge(silu_done, i * 2 + (j0 + s + 1))
                            dve.tensor_tensor(stage2[s][:, :], stage2[s][:, :],
                                              ps[:, 2:4, :].rearrange("p a n -> p (a n)"),
                                              ALU.mult).then_inc(hid_mult, 1)
                            dve.wait_ge(hid_high, i * 2 + (j0 + s + 1))
                            hid = ds(i * 2 + s, 1)
                            dve.tensor_tensor(act_lo[:, hid, :].rearrange("p a n -> p (a n)"), stage2[s][:, :],
                                              act_hi[:, hid, :].rearrange("p a n -> p (a n)").bitcast(f32),
                                              ALU.subtract).then_inc(hid_ready, 1)

                def add_y(m, b, count):
                    dve.wait_ge(y_turned, count)
                    dst = x2[:, :, ds(m * P, P)]
                    pair = (b % 2) * 2
                    dve.tensor_tensor(dst, dst, ps[:, pair:pair + 2, :].rearrange("p a (t n) -> p (a t) n", n=P),
                                      ALU.add).then_inc(x2_added, 1)

                def down_item(b, rnd, split):
                    n = n0 + 2 * g + b
                    dve.wait_ge(gemm_done, rnd * 4 + (n + 1 - GEMM_LAG))
                    if split:
                        ffn_split_lo(n + 2, rnd * 4 + (n + 3 - GEMM_LAG))

                if gi < len(FFN_PLAN) - 1:
                    with dve.Fori(0, KT // 4) as i:
                        for b in range(4):
                            down_item(b, i, True)
                            if b >= 1:
                                add_y(i * 4 + (b - 1), b - 1, i * 4 + (gi * KT + b))
                        add_y(i * 4 + 3, 3, i * 4 + (gi * KT + 4))
                else:
                    for m in range(KT):
                        down_item(m, 0, m + 2 < KT)
                        if m >= 1:
                            add_y(m - 1, m - 1, gi * KT + m)
                    add_y(KT - 1, KT - 1, gi * KT + KT)

        @block.tensor
        def _(pe):
            pe.wait_ge(consts_ready, 1)
            pe.wait_ge(pos_float, 1)
            pe.transpose(ps[:, 7, 0:C_POS], rows, ident[0:C_POS, 0:C_POS])
            pe.transpose(ps[:, 7, C_POS:C_POS + TT], pos_f, ident[0:TT, 0:TT]).then_inc(cols_in_psum, 1)
            for t in range(TT):
                pe.wait_ge(raw_used, t + 1)
                if t >= 2:
                    pe.wait_ge(bank_pair_free, t - 1)
                for k in range(KT):
                    last = pe.transpose(ps[:, (t % 2) * 2 + k // 4, (k % 4) * P:(k % 4 + 1) * P],
                                        x_scaled[t % 2][:, k * P:(k + 1) * P], ident[:, :])
                last.then_inc(x_turned, 1)

            def gemm(whi, wlo, a_hi, a_lo, pair, kts, signal, rows=P, tail=None, late_half=None):
                passes = [(0,), (1,)] if late_half else [(0, 1)]
                for halves in passes:
                    if halves == (1,):
                        pe.wait_ge(*late_half)
                    for k in range(kts):
                        if tail and k == kts - 1:
                            pe.wait_ge(*tail)
                        for w, moving in ((whi, (a_hi, a_lo)), (wlo, (a_hi,))):
                            for a in moving:
                                for h in halves:
                                    last = pe.matmul(ps[0:rows, pair + h, :], w[:, k, 0:rows],
                                                     a[:, k, h * BANK:(h + 1) * BANK],
                                                     start=(k == 0 and w is whi and a is a_hi),
                                                     stop=(k == kts - 1 and w is wlo))
                last.then_inc(signal, 1)

            pe.wait_ge(h_ready, TT // 2)
            pe.wait_ge(raw_used, N_X + 1)
            gemm(w_hi[0], w_lo[0], act_hi, act_lo, 0, KT, gemm_done, SMALL, late_half=(h_ready, TT))
            for m in range(1, M_QKV):
                pe.wait_ge(raw_used, N_X + m + 1)
                pe.wait_ge(bank_pair_free, TT + m - 1)
                gemm(w_hi[m % 2], w_lo[m % 2], act_hi, act_lo, (m % 2) * 2, KT, gemm_done)
                if m == 1:
                    pe.wait_ge(bank_pair_free, TT + 1)
                    for t in range(TT):
                        last = pe.transpose(ps[:, 6, t * SMALL:(t + 1) * SMALL], smallT[:, t * P:(t + 1) * P],
                                            ident[0:SMALL, 0:SMALL])
                    last.then_inc(small_turned, 1)
                if m == M_SMALL + 2:
                    pe.wait_ge(mid_dve.sem, mid_dve.after("g"))
                    for j, tri in enumerate((le, gt, ones)):
                        last = pe.matmul(ps[:, 6, j * 32:(j + 1) * 32], tri[:, :],
                                         g_log[:, :, :].rearrange("p t h -> p (t h)"), start=True, stop=True)
                    last.then_inc(mid_pe.sem, 1)
                if m == M_QKV - 1:
                    pe.wait_ge(lat_squared, 3)
                    for t in range(TT):
                        for k in range(3):
                            last = pe.matmul(ps[:, 5, 2 * t + k // 2:2 * t + k // 2 + 1],
                                             c_sq[:, k, t * P:(t + 1) * P], ones[:, 0:1],
                                             start=(k != 1), stop=(k != 0))
                    last.then_inc(lat_summed, 1)
            with pe.Fori(0, QKV_TILES // 4) as i:
                for b in range(4):
                    m = M_QKV + b
                    pe.wait_ge(raw_used, i * 4 + (N_X + m + 1))
                    pe.wait_ge(bank_pair_free, i * 4 + (TT + m - 1))
                    gemm(w_hi[m % 2], w_lo[m % 2], act_hi, act_lo, (m % 2) * 2, KT, gemm_done)
            pe.wait_ge(bank_pair_free, TT + M_QKV + 1)
            pe.wait_ge(pw_loaded, (POOL_GROUPS + 2) * 16)
            pe.wait_ge(mid_act.sem, mid_act.after("decays"))
            for p in range(2):
                for h in range(HALVES):
                    last = pe.matmul(ps[:, 4 + 2 * p + h, :], pw[:, p, :], pz[:, p, h * BANK:(h + 1) * BANK],
                                     start=True, stop=True)
                last.then_inc(mid_pe.sem, 1)
            for m in range(M_GATE, IN_ALL):
                pe.wait_ge(raw_used, N_X + m + 1)
                if m < M_GATE + 2:
                    pe.wait_ge(bank_pair_free, TT + m - 1)
                else:
                    pe.wait_ge(gate_pair_free, m - M_GATE - 1)
                gemm(w_hi[m % 2], w_lo[m % 2], act_hi, act_lo, (m % 2) * 2, KT, gemm_done)

            pe.wait_ge(gate_pair_free, GATE_TILES)
            pe.wait_ge(raw_used, N_X + IN_ALL)
            pe.wait_ge(mla_weights, 1)
            pe.wait_ge(mid_act.sem, mid_act.after("pool1"))

            pe.sem_inc(mla_pe.sem, mla_pe.base)
            with pe.Fori(0, TT // 4) as i:
                for b in range(4):
                    pe.wait_ge(mla_act.sem, mla_act.after(f"cTf{b}", i))
                    pe.wait_ge(mla_act.sem, mla_act.after(f"turned{b}", i - 1))
                    for k in range(2):
                        pe.matmul(ps[:, 2 * b, 0:HEADS * QK], cTf[b][:, k, :], wuq[:, k, :],
                                  start=(k == 0), stop=(k == 1))
                    pe.matmul(ps[:, 2 * b + 1, :], cTf[b][:, 2, :], wukv[:, :], start=True,
                              stop=True).then_inc(mla_pe.sem, 1)
                for b in range(4):
                    pe.wait_ge(mla_dve.sem, mla_dve.after(f"qk{b}", i))
                    for h in range(HEADS):
                        pe.transpose(ps[0:QK, 2 * b, h * P:(h + 1) * P], qk[b][:, 0, h, :], ident[:, :])
                        last = pe.transpose(ps[0:QK, 2 * b + 1, h * P:(h + 1) * P], qk[b][:, 1, h, :], ident[:, :])
                    last.then_inc(mla_pe.sem, 1)

            for c_ in (gp[0], gp[1], tp):
                pe.sem_inc(c_.sem, len(c_.names))
            pe.wait_ge(mla_act.sem, mla_act.after("turned3", TT // 4 - 1))
            pe.wait_ge(mid_act.sem, mid_act.after("decays"))
            def stages(order, rnd):
                def gafter(c, name, rnd=None):
                    pe.wait_ge(c.sem, c.after(name, i if rnd is None else rnd))

                def four(out_bank, lhs, rhs, counter):
                    for h in range(4):
                        last = pe.matmul(ps[:, out_bank, h * P:(h + 1) * P], lhs(h), rhs(h), start=True, stop=True)
                    last.then_inc(counter.sem, 1)

                def four_t(out_bank, src, counter):
                    for h in range(4):
                        last = pe.transpose(ps[:, out_bank, h * P:(h + 1) * P], src(h), ident[:, :])
                    last.then_inc(counter.sem, 1)

                for stage_name, b, back in order:
                    i = rnd - back
                    if stage_name in GDN_STAGES:
                        q = lambda h: qkvf[b][:, h, :]
                        k = lambda h: qkvf[b][:, 4 + h, :]
                        x1 = lambda h: qkvf[b][:, 8 + h, :]
                        on = lambda t3: (lambda h: t3[:, h, :])
                        n_ = lambda p: (lambda h: N_[b][:, p, h, :])
                        cnt = gp[b]
                    if stage_name == "decay":
                        gafter(gd[b], "gtg")
                        four(U[b], on(B_[b]), lambda h: le[:, :], cnt)
                        gafter(ga[b], "sq")
                        for h in range(8):
                            last = pe.matmul(ps[:, W[b], h:h + 1], N_[b][:, h // 4, h % 4, :], ones[:, 0:1],
                                             start=True, stop=True)
                        last.then_inc(cnt.sem, 1)
                    elif stage_name == "kk":
                        gafter(ga[b], "exp")
                        four(U[b], k, k, cnt)
                        gafter(gd[b], "ss")
                        four(W[b], k, q, cnt)
                    elif stage_name == "turn":
                        gafter(gd[b], "att")
                        four_t(W[b], k, cnt)
                        gafter(gd[b], "a0")
                        four_t(U[b], x1, cnt)
                    elif stage_name == "m0":
                        gafter(gd[b], "n0")
                        gafter(gd[b], "kd")
                        four_t(W[b], n_(0), cnt)
                    elif stage_name in X_STAGES:
                        l = int(stage_name[1:])
                        gafter(gg[b], f"b{l}")
                        if l == 1:
                            gafter(ga[b], "m0")
                            gafter(gd[b], "vn")
                        else:
                            gafter(gd[b], f"m{l - 1}")
                        four(U[b], on(B_[b]), on(M_[b]), cnt)
                    elif stage_name in YZ_STAGES:
                        l = int(stage_name[2:])
                        gafter(ga[b], f"x{l}")
                        four(W[b], x1, n_((l - 1) % 2), cnt)
                        if l < LAST:
                            four(U[b], n_((l - 1) % 2), x1, cnt)
                    elif stage_name == "ks":
                        gafter(gd[1 - b], "s", i - 1 if b == 0 else i)
                        gafter(gd[b], f"n{LAST}")
                        four(U[b], k, on(S_), cnt)
                        four(W[b], q, on(S_), cnt)
                    elif stage_name == "tr":
                        gafter(gd[b], "r")
                        four(U[b], n_(0), on(E_[b]), cnt)
                    elif stage_name == "av":
                        gafter(gd[b], "v")
                        four(U[b], on(attn[b]), on(A_[b]), cnt)
                        four(W[b], on(kd[b]), on(A_[b]), cnt)
                    elif stage_name == "ot":
                        gafter(gd[b], "on")
                        four_t(U[b], n_(1), cnt)
                    elif stage_name == "att_s":
                        t, w = b, (b + 1) * P
                        if t == TT - 1:
                            pe.wait_ge(head_loaded, i * 16 + 16)
                            gafter(ta, "e0", i - 1)
                        else:
                            gafter(ta, f"e{t + 1}")
                        for h in range(-(-w // BANK)):
                            n = min(BANK, w - h * BANK)
                            last = pe.matmul(ps[:, 4 + h, 0:n], qh[0:QK, t * P:(t + 1) * P],
                                             kT[0:QK, ds(i, 1), h * BANK:h * BANK + n].rearrange("p a n -> p (a n)"),
                                             start=True, stop=True)
                        last.then_inc(tp.sem, 1)
                    elif stage_name == "att_t":
                        t, g = b
                        if g == 0:
                            gafter(ta, f"e{t}")
                            if t < TT - 1:
                                gafter(ta, f"p{t + 1}.{t + 1 >= 4:d}")
                            else:
                                gafter(ta, "p0.0", i - 1)
                        else:
                            gafter(ta, f"p{t}.0")
                        for j in range(min(4, t + 1 - 4 * g)):
                            kt = 4 * g + j
                            last = pe.transpose(ps[:, 6, j * P:(j + 1) * P], probs[:, kt * P:(kt + 1) * P], ident[:, :])
                        last.then_inc(tp.sem, 1)
                    elif stage_name == "att_pv":
                        t, g = b
                        gafter(ta, f"p{t}.{g}")
                        if g == 0:
                            if t < TT - 1:
                                gafter(td, f"o{t + 1}")
                            else:
                                gafter(td, "o0", i - 1)
                        for j in range(min(4, t + 1 - 4 * g)):
                            kt = 4 * g + j
                            last = pe.matmul(ps[:, 7, 0:V_DIM], probsT[0][:, j, :],
                                             V[:, kt, ds(i, 1), :].rearrange("p a d -> p (a d)"),
                                             start=(kt == 0), stop=(kt == t))
                        last.then_inc(tp.sem, 1)

            stages(FIRST_ROUND, 0)
            with pe.Fori(1, TT // 2) as rnd:
                stages(ORDER, rnd)
            pe.wait_ge(td.sem, td.after("o0", TT // 2 - 1))
            pe.wait_ge(ta.sem, ta.after("p0.0", TT // 2 - 1))
            for q4 in range(4):
                for j in range(2):
                    for t2 in range(2):
                        last = pe.transpose(ps[:, 4 + q4, (2 * j + t2) * P:(2 * j + t2 + 1) * P],
                                            V[:, 2 * q4 + t2, 2 * j:2 * j + 2, :].rearrange("p h d -> p (h d)"),
                                            ident[:, :])
                last.then_inc(att_turned, 1)

            def out_product(t, k):
                for h in range(HALVES):
                    last = pe.matmul(ps[:, op_pair[t] + h, :], oT[:, k, t * P:(t + 1) * P],
                                     w_out_sb[:, k, h * BANK:(h + 1) * BANK], start=(k == 0), stop=(k == KT - 1))
                if k == KT - 1:
                    last.then_inc(op_done, 1)

            pe.wait_ge(gd[0].sem, gd[0].after("out", TT // 2 - 1))
            pe.wait_ge(gd[1].sem, gd[1].after("out", TT // 2 - 2))
            pe.wait_ge(att_moved, 4)
            per_stage = len(OP_EARLY) // len(AFTER_ROUNDS)
            assert per_stage * len(AFTER_ROUNDS) == len(OP_EARLY)
            for n, stage in enumerate(AFTER_ROUNDS):
                stages([stage], TT // 2)
                for t, k in OP_EARLY[n * per_stage:(n + 1) * per_stage]:
                    if t == 0 and k % 4 == 0:
                        pe.wait_ge(w_out_loaded[k // 4], 4 * 16)
                    out_product(t, k)

            pe.wait_ge(gd[1].sem, gd[1].after("out", TT // 2 - 1))

            def turn_x2(t):
                pe.wait_ge(x2_scaled, t + 1)
                if t >= 2:
                    pe.wait_ge(raw_used, N_X2 + t - 1)
                rows_t = raw[(N_X2 + t) % RAW]
                for k in range(KT):
                    last = pe.transpose(ps[:, 4 + (t % 2) * 2 + k // 4, (k % 4) * P:(k % 4 + 1) * P],
                                        rows_t[:, k, :], ident[:, :])
                last.then_inc(x2_turned, 1)

            for t in range(2, TT):
                if t == 3:
                    pe.wait_ge(x2_ready, 1)
                elif t > 3:
                    pe.wait_ge(x2_ready, t - 1)
                for k in range(KT):
                    out_product(t, k)
                for turned in {2: (0,), 3: (1, 2)}.get(t, (t - 1,)):
                    turn_x2(turned)
            turn_x2(TT - 1)

            pe.wait_ge(hf_ready, TT // 2)
            for gi, (n0, j0, g) in enumerate(FFN_PLAN):
                with pe.Fori(0, g // 2) as i:
                    for b in range(4):
                        n, s = n0 + b, b // 2
                        pe.wait_ge(raw_used, i * 4 + (n + 1))
                        if b % 2 == 0:
                            pe.wait_ge(silu_done, i * 2 + (j0 + s))
                        else:
                            pe.wait_ge(hid_mult, i * 2 + (j0 + s))
                        if gi > 0 and b < 2:
                            pe.wait_ge(x2_added, gi * KT)
                        gemm(w_hi[n % 2], w_lo[n % 2], hf_hi, hf_lo, (b % 2) * 2, KT, gemm_done,
                             late_half=(hf_ready, TT) if gi == 0 and b == 0 else None)

                def down_gemm(b, rnd):
                    n = n0 + 2 * g + b
                    pe.wait_ge(raw_used, rnd * 4 + (n + 1))
                    if b == 0:
                        pe.wait_ge(hid_ready, j0 + g - 1)
                    if gi > 0 or b >= 2:
                        pe.wait_ge(y_copied, rnd * 4 + (gi * KT + b - 1))
                    elif not isinstance(rnd, int):
                        pe.wait_ge(y_copied, rnd * 4 + 0)
                    gemm(w_hi[n % 2], w_lo[n % 2], act_hi, act_lo, 4 + (b % 2) * 2, g, gemm_done,
                         tail=(hid_ready, j0 + g) if b == 0 else None)

                def turn_y(b, rnd):
                    pe.wait_ge(y_copied, rnd * 4 + (gi * KT + b + 1))
                    if gi > 0 or b >= 2:
                        pe.wait_ge(x2_added, rnd * 4 + (gi * KT + b - 1))
                    elif not isinstance(rnd, int):
                        pe.wait_ge(x2_added, rnd * 4 + 0)
                    for t in range(TT):
                        last = pe.transpose(ps[:, (b % 2) * 2 + t // 4, (t % 4) * P:(t % 4 + 1) * P],
                                            stage2[b % 2][:, t * P:(t + 1) * P], ident[:, :])
                    last.then_inc(y_turned, 1)

                if gi < len(FFN_PLAN) - 1:
                    with pe.Fori(0, KT // 4) as i:
                        for b in range(4):
                            down_gemm(b, i)
                            if b >= 1:
                                turn_y(b - 1, i)
                        turn_y(3, i)
                else:
                    for m in range(KT):
                        down_gemm(m, 0)
                        if m >= 1:
                            turn_y(m - 1, 0)
                    turn_y(KT - 1, 0)



_INS = ["x", "positions", "attn_norm", "w_in", "conv_w", "a_log", "dt_bias", "gdn_out_norm", "pool_w", "pool_scale",
        "q_a_norm", "w_uq", "kv_a_norm", "w_ukv", "q_norm", "k_norm", "w_out", "ffn_norm", "w_gate_up", "w_down"]


def kernel(**inputs):
    import concourse.bacc as bacc
    from concourse.bass_utils import run_bass_kernel_spmd

    nc = bacc.Bacc("TRN2", target_bir_lowering=False, num_devices=1)
    arrays, args = {}, []
    for name in _INS:
        a = np.ascontiguousarray(inputs[name])
        arrays[f"in_{name}"] = a
        args.append(nc.dram_tensor(f"in_{name}", a.shape, mybir.dt.from_np(a.dtype), kind="ExternalInput").ap())
    out = nc.dram_tensor("out_0", (1, SEQ, D_MODEL), mybir.dt.float32, kind="ExternalOutput").ap()
    hybrid_block(nc, *args, out)
    result = run_bass_kernel_spmd(nc, [arrays], core_ids=[0])
    return result.results[0]["out_0"]
```
